# Optimizing a Trainium2 kernel written in Bass

```python
import jax, jax.numpy as jnp
from jax import lax
import numpy as np

D_MODEL = 1024
BATCH = 1
SEQ = 256
DEPTH = 2

ATT_HEADS = 4
D_ATT = D_MODEL // 2
ATT_DV = D_ATT // ATT_HEADS
ATT_DK = ATT_DV // 2
CC_CH = D_MODEL // 4
CC_GROUPS = 4
CC_K = 31
SC_CH = D_MODEL // 4
SC_K = 3
D_MIX = D_ATT + CC_CH + SC_CH
Q_COLS = ATT_HEADS * 2 * ATT_DK
K_COLS = ATT_HEADS * 2 * ATT_DK
V_COLS = ATT_HEADS * ATT_DV
CC_COLS = 2 * CC_CH
SC_COLS = 3 * SC_CH
D_IN = Q_COLS + K_COLS + V_COLS + CC_COLS + SC_COLS
D_FF = ((8 * D_MODEL // 3 + 255) // 256) * 256
MEM_LEN = 256
XA_HEADS = 4
XA_HD = D_MODEL // XA_HEADS
Q_BLOCK = 128
EPS = 1e-6

kernel_name = "hymba_style_diffattn_conformer_shortconv_hybrid"

def rms_norm(x, g):
    xf = x.astype(jnp.float32)
    y = xf * lax.rsqrt(jnp.mean(xf * xf, axis=-1, keepdims=True) + EPS)
    return (y * g.astype(jnp.float32)).astype(x.dtype)

def layer_norm(x, g, b):
    xf = x.astype(jnp.float32)
    mu = jnp.mean(xf, axis=-1, keepdims=True)
    var = jnp.mean(jnp.square(xf - mu), axis=-1, keepdims=True)
    y = (xf - mu) * lax.rsqrt(var + EPS)
    return (y * g.astype(jnp.float32) + b.astype(jnp.float32)).astype(x.dtype)

def swiglu(h, w_gate, w_up, w_down):
    return (jax.nn.silu(h @ w_gate) * (h @ w_up)) @ w_down

def causal_depthwise_conv(u, w):
    k_w, c = w.shape
    return lax.conv_general_dilated(
        u, w[:, None, :].astype(u.dtype), window_strides=(1,), padding=[(k_w - 1, 0)],
        dimension_numbers=("NWC", "WIO", "NWC"), feature_group_count=c)

def diff_attention(q, k, v, lam, slopes):
    b, t = q.shape[0], q.shape[1]
    n_blocks = t // Q_BLOCK
    kpos = jnp.arange(t)
    scale = ATT_DK ** -0.5

    def block(i):
        start = i * Q_BLOCK
        qb = lax.dynamic_slice_in_dim(q, start, Q_BLOCK, axis=1)
        s = jnp.einsum("bqhcd,bkhcd->bhcqk", qb, k).astype(jnp.float32) * scale
        dist = (start + jnp.arange(Q_BLOCK))[:, None] - kpos[None, :]
        bias = -slopes[:, None, None] * dist.astype(jnp.float32)[None]
        s = jnp.where((dist >= 0)[None, None, None], s + bias[None, :, None], -jnp.inf)
        p = jax.nn.softmax(s, axis=-1)
        a = p[:, :, 0] - lam * p[:, :, 1]
        return jnp.einsum("bhqk,bkhd->bqhd", a.astype(v.dtype), v)

    out = lax.map(block, jnp.arange(n_blocks))
    return jnp.moveaxis(out, 0, 1).reshape(b, t, ATT_HEADS, ATT_DV)

def setup_inputs(seed: int = 0) -> dict:
    key = jax.random.key(seed)
    ks = iter(jax.random.split(key, 40))

    def nrm(shape, scale):
        return jax.random.normal(next(ks), shape, jnp.float32) * scale

    def gain(shape):
        return 1.0 + nrm(shape, 0.02)

    L, D, F = DEPTH, D_MODEL, D_FF
    return {
        "x": nrm((BATCH, SEQ, D), 1.0),
        "mem": nrm((BATCH, MEM_LEN, D), 1.0),
        "ffn1_norm": gain((L, D)),
        "ffn1_w_gate": nrm((L, D, F), D ** -0.5),
        "ffn1_w_up": nrm((L, D, F), D ** -0.5),
        "ffn1_w_down": nrm((L, F, D), F ** -0.5),
        "mix_norm": gain((L, D)),
        "w_in": nrm((L, D, D_IN), D ** -0.5),
        "lam_q1": nrm((L, ATT_DK), 0.1),
        "lam_k1": nrm((L, ATT_DK), 0.1),
        "lam_q2": nrm((L, ATT_DK), 0.1),
        "lam_k2": nrm((L, ATT_DK), 0.1),
        "diff_subln": gain((L, ATT_DV)),
        "cc_dw": nrm((L, CC_K, CC_CH), CC_K ** -0.5),
        "cc_dw_b": nrm((L, CC_CH), 0.01),
        "cc_ln_g": gain((L, CC_CH)),
        "cc_ln_b": nrm((L, CC_CH), 0.01),
        "sc_dw": nrm((L, SC_K, SC_CH), SC_K ** -0.5),
        "w_out": nrm((L, D_MIX, D), D_MIX ** -0.5),
        "xa_norm": gain((L, D)),
        "mem_norm": gain((L, D)),
        "xa_wq": nrm((L, D, XA_HEADS * XA_HD), D ** -0.5),
        "xa_wkv": nrm((L, D, 2 * XA_HEADS * XA_HD), D ** -0.5),
        "xa_wo": nrm((L, XA_HEADS * XA_HD, D), D ** -0.5),
        "ffn2_norm": gain((L, D)),
        "ffn2_w_gate": nrm((L, D, F), D ** -0.5),
        "ffn2_w_up": nrm((L, D, F), D ** -0.5),
        "ffn2_w_down": nrm((L, F, D), F ** -0.5),
        "final_norm": gain((D,)),
    }

def reference(x, mem, ffn1_norm, ffn1_w_gate, ffn1_w_up, ffn1_w_down, mix_norm, w_in,
              lam_q1, lam_k1, lam_q2, lam_k2, diff_subln, cc_dw, cc_dw_b, cc_ln_g, cc_ln_b,
              sc_dw, w_out, xa_norm, mem_norm, xa_wq, xa_wkv, xa_wo, ffn2_norm, ffn2_w_gate,
              ffn2_w_up, ffn2_w_down, final_norm):
    b, t, _ = x.shape
    slopes = 2.0 ** (-8.0 * jnp.arange(1, ATT_HEADS + 1, dtype=jnp.float32) / ATT_HEADS)

    for l in range(DEPTH):
        x = x + 0.5 * swiglu(rms_norm(x, ffn1_norm[l]), ffn1_w_gate[l], ffn1_w_up[l], ffn1_w_down[l])

        z = rms_norm(x, mix_norm[l]) @ w_in[l]
        zq, zk, zv, zc, zs = jnp.split(
            z, np.cumsum([Q_COLS, K_COLS, V_COLS, CC_COLS])[:].tolist(), axis=-1)

        lam_init = 0.8 - 0.6 * float(np.exp(-0.3 * l))
        lam = (jnp.exp(jnp.sum(lam_q1[l].astype(jnp.float32) * lam_k1[l].astype(jnp.float32)))
               - jnp.exp(jnp.sum(lam_q2[l].astype(jnp.float32) * lam_k2[l].astype(jnp.float32)))
               + lam_init)
        q = zq.reshape(b, t, ATT_HEADS, 2, ATT_DK)
        k = zk.reshape(b, t, ATT_HEADS, 2, ATT_DK)
        v = zv.reshape(b, t, ATT_HEADS, ATT_DV)
        o_att = diff_attention(q, k, v, lam, slopes)
        o_att = (rms_norm(o_att, diff_subln[l]) * (1.0 - lam_init)).reshape(b, t, D_ATT)

        ca, cg = jnp.split(zc, 2, axis=-1)
        u = ca * jax.nn.sigmoid(cg)
        u = causal_depthwise_conv(u, cc_dw[l]) + cc_dw_b[l]
        o_cc = jax.nn.silu(layer_norm(u, cc_ln_g[l], cc_ln_b[l]))

        gb, gc, hs = jnp.split(zs, 3, axis=-1)
        o_sc = gb * causal_depthwise_conv(gc * hs, sc_dw[l])

        x = x + jnp.concatenate([o_att, o_cc, o_sc], axis=-1) @ w_out[l]

        hq = (rms_norm(x, xa_norm[l]) @ xa_wq[l]).reshape(b, t, XA_HEADS, XA_HD)
        kv = rms_norm(mem, mem_norm[l]) @ xa_wkv[l]
        mk, mv = jnp.split(kv.reshape(b, MEM_LEN, 2, XA_HEADS, XA_HD), 2, axis=2)
        mk, mv = mk[:, :, 0], mv[:, :, 0]
        s = jnp.einsum("bqhd,bmhd->bhqm", hq, mk).astype(jnp.float32) * (XA_HD ** -0.5)
        p = jax.nn.softmax(s, axis=-1).astype(mv.dtype)
        o = jnp.einsum("bhqm,bmhd->bqhd", p, mv).reshape(b, t, XA_HEADS * XA_HD)
        x = x + o @ xa_wo[l]

        x = x + 0.5 * swiglu(rms_norm(x, ffn2_norm[l]), ffn2_w_gate[l], ffn2_w_up[l], ffn2_w_down[l])

    return rms_norm(x, final_norm)


_drawn_inputs = setup_inputs


def setup_inputs(seed=0):
    import zlib

    import numpy as np

    out = dict(_drawn_inputs(seed))
    spreads = {}
    factors = {'ffn1_norm': 3.739,
     'lam_q1': 3.103,
     'lam_k2': 2.801,
     'diff_subln': 4.854,
     'cc_dw_b': 7.347,
     'cc_ln_g': 6.607,
     'cc_ln_b': 8.0,
     'xa_norm': 8.0,
     'mem_norm': 8.0,
     'ffn2_norm': 6.05,
     'final_norm': 2.745}
    for name, (base, spread) in spreads.items():
        noise = np.random.default_rng([zlib.crc32(name.encode()), seed]).standard_normal(out[name].shape)
        drawn = base * np.exp(spread * noise) if base else spread * noise
        out[name] = __import__('jax').numpy.asarray(drawn.astype(out[name].dtype))
    for name, factor in factors.items():
        out[name] = (out[name] * factor).astype(out[name].dtype)
    return out
```

```python
from contextlib import ExitStack

import concourse.bass as bass
from concourse import mybir

F32 = mybir.dt.float32
F32R = mybir.dt.float32r
BF16 = mybir.dt.bfloat16
ALU = mybir.AluOpType
ACT = mybir.ActivationFunctionType
AX_X = mybir.AxisListType.X

P = 128
EPS = 1e-6
NORMS = ("ffn1_norm", "mix_norm", "xa_norm", "ffn2_norm", "mem_norm")

D, T, L, F = 1024, 256, 2, 2816
HEADS, DK, DV = 4, 64, 128
CC, KC, KS = 256, 31, 3
XH, XD = 4, 256
KD = D // P
TT = T // P
N = 512
CF = N // 2
STEPS = F // CF
BLOCK = 2048
SLOTS = 3
FIRST = 1

FFN_BLOCKS = 3 * STEPS
B_FFN1 = 0
B_IN = B_FFN1 + FFN_BLOCKS
B_KV = B_IN + 11
B_OUT = B_KV + 8
B_Q = B_OUT + 4
B_O = B_Q + 4
B_FFN2 = B_O + 4
NB = B_FFN2 + FFN_BLOCKS
OUT_ORDER = (2, 3, 0, 1)

C_GAIN = 0
C_SUB = C_GAIN + 8 * len(NORMS)
C_CCW = C_SUB + 1
C_CCB = C_CCW + 2 * KC
C_LNG = C_CCB + 2
C_LNB = C_LNG + 2
C_SCW = C_LNB + 2
C_LAM = C_SCW + 2 * KS
C_INIT = C_LAM + 4 * DK
C_REST = C_INIT + 1
NPAR = C_REST + 1

K_ID = 0
K_MEAN = K_ID + P
K_DIST = K_MEAN + P
NCONST = K_DIST + TT * T
MASKED = 1e38


class Signals:

    def __init__(self, sem, events):
        self.sem, self.order, self.n, self.next = sem, {e: i for i, e in enumerate(events)}, len(events), 0
        assert len(self.order) == self.n

    def one(self, event):
        assert self.order[event] == self.next % self.n, event
        self.next += 1
        return 1

    def at(self, layer, event):
        return layer * self.n + self.order[event] + 1


def hymba_kernel(nc, x_d, mem_d, memT_d, w_d, par_d, const_d, fin_d, out_d):
    ctx = ExitStack()
    with ctx:
        def sb(name, shape, dt=F32):
            return ctx.enter_context(nc.sbuf_tensor(name, shape, dt))

        def sem(name):
            return ctx.enter_context(nc.semaphore(name))

        def signals(name, events):
            return Signals(sem(name), events)

        w_raw = sb("w_raw", [P, SLOTS, BLOCK])
        w_hi = sb("w_hi", [P, SLOTS, BLOCK], F32R)
        w_lo = sb("w_lo", [P, SLOTS, BLOCK], F32R)
        x = sb("x", [P, TT, D])
        a_hi = sb("a_hi", [P, KD, T], F32R)
        a_lo = sb("a_lo", [P, KD, T], F32R)
        m_hi = sb("m_hi", [P, KD, T], F32R)
        m_lo = sb("m_lo", [P, KD, T], F32R)
        hT_hi = sb("hT_hi", [P, 2, T], F32R)
        hT_lo = sb("hT_lo", [P, 2, T], F32R)
        const = sb("const", [P, NCONST])
        ident = const[:, K_ID:K_ID + P]
        mean_w = const[:, K_MEAN:K_MEAN + P]
        par = sb("par", [P, NPAR])
        zeros = sb("zeros", [P, N], BF16)
        half = sb("half", [P, 8])
        over_d = sb("over_d", [P, 8])
        over_dv = sb("over_dv", [P, 8])
        eps = sb("eps", [P, 1])
        ssq = sb("ssq", [P, TT])
        var = sb("var", [P, TT])
        rinv = sb("rinv", [P, TT])
        nrinv = sb("nrinv", [P, TT])
        ssm = sb("ssm", [P, TT])
        rmem = sb("rmem", [P, TT])
        junk = sb("junk", [P, D])
        zqk = sb("zqk", [P, 2, TT, N])
        qkT = sb("qkT", [P, 2 * HEADS, T])
        hq = zqk[:, :, :, :].rearrange("p a t n -> p (a t n)").rearrange("p (t n) -> p t n", t=TT)
        hqT = qkT
        v_sb = sb("v_sb", [P, TT, N])
        u_sb = sb("u_sb", [P, TT, CC])
        gbc = sb("gbc", [P, TT, N])
        gch = sb("gch", [P, TT, CC])
        sig = sb("sig", [P, TT, CC])
        u_pad = sb("u_pad", [P, 2, KC - 1 + T])
        s_pad = sb("s_pad", [P, 2, KS - 1 + T])
        gbT = sb("gbT", [P, 2, T])
        acc = sb("acc", [P, 2, T])
        accs = sb("accs", [P, 2, T])
        sq = sb("sq", [P, 2, T])
        rstd = sb("rstd", [P, T])
        s_sb = sb("s_sb", [P, 2, T])
        e_sb = sb("e_sb", [P, 2, 2, T])
        prob = sb("prob", [P, T])
        probT = sb("probT", [P, 2, P])
        o_sb = sb("o_sb", [P, HEADS, DV])
        on_sb = sb("on_sb", [P, TT, HEADS, DV])
        sg = sig
        h_sb = u_sb
        kx = sb("kx", [P, TT, D])
        m_raw = kx[:, :, :].rearrange("p t n -> p (t n)").rearrange("p (k m) -> p k m", k=KD)
        vx = sb("vx", [P, TT, D])
        kxT = sb("kxT", [P, KD, T])
        e_x = e_sb[:, :, 0, :]
        o_x = s_sb
        mx = sb("mx", [P, 2])
        nmx = sb("nmx", [P, 2, 2])
        den = sb("den", [P, 2, 2])
        rden = sb("rden", [P, 2])
        sso = sb("sso", [P, TT, HEADS])
        varo = sb("varo", [P, TT, HEADS])
        ro = sb("ro", [P, TT, HEADS])
        lam2 = sb("lam2", [P, 2])
        elam = sb("elam", [P, 2])
        lam = sb("lam", [P, 1])
        gsub = sb("gsub", [P, 1])
        fing = kxT[:, 0:4, :].rearrange("p k m -> p (k m)")
        y = vx

        G = [ctx.enter_context(nc.psum_tensor(f"G{i}", [P, N], F32)) for i in range(4)]
        DB = [ctx.enter_context(nc.psum_tensor(f"D{i}", [P, N], F32)) for i in range(4)]

        s_x = sem("x_loaded")
        s_const = sem("const_loaded")
        s_mem = sem("mem_loaded")
        s_fing = sem("final_gain_loaded")
        s_par = sem("params_loaded")
        s_mraw = sem("memT_loaded")
        s_out = sem("out_stored")
        w_in = [sem(f"w_loaded{i}") for i in range(SLOTS)]
        s_hi = sem("w_hi_ready")
        s_lo = sem("w_lo_ready")
        s_blk = sem("block_multiplied")
        s_init = sem("constants_set")
        s_rmem = sem("rmem_ready")
        s_ssm = sem("ssm_ready")
        s_xup = sem("x_updated")
        s_xT = sem("xT_in_psum")
        s_ahi = sem("a_hi_ready")
        s_alo = sem("a_lo_ready")
        s_ssq = sem("ssq_ready")
        s_rinv = sem("rinv_ready")
        s_silu = sem("silu_ready")
        s_h = sem("h_ready")
        s_hT = sem("hT_in_psum")
        s_hhi = sem("hT_hi_ready")
        s_hlo = sem("hT_lo_ready")
        s_fin = sem("final_ready")
        mm_ = signals("mem_ready", ["hi", "lo"])
        conv_pe = signals("conv_pe", ["uT", "sT", "gbT", "mean", "var"])
        conv_act = signals("conv_act", ["ecg", "uT", "gbc", "sT", "gbT", "std", "esilu", "cchi", "schi"])
        conv_dve = signals("conv_dve", ["u", "gch", "acc", "sq", "norm", "cc", "cclo", "sc", "sclo"])
        units = range(TT * HEADS)
        att_pe = signals("att_pe", ["qT0", "qT1", "kT0", "kT1", "S0", "S1"] + [
            f"{e}{u + d}" for u in units for e, d in (("pv", -1), ("aT", 0), ("S", 2))
            if 0 <= u + d < len(units) and f"{e}{u + d}" != "pv7"] + ["pv7", "kx0", "oT0", "oT1", "kx1"])
        att_act = signals("att_act", ["elam", "q", "qT", "k", "kT", "v", "exp0"] + [
            e for u in units for e in
            ([f"exp{u + 1}"] if u + 1 < len(units) else []) + [f"aT{u}"] + (["o0"] if u == 4 else [])
            + ([f"kv{u // 2}"] if u % 2 else [])] + ["o1", "kx0", "oT0", "oT1", "kx1"])
        att_dve = signals("att_dve", ["lam2", "lam", "max0"] + [
            e for u in units for e in
            [f"a{u}"] + ([f"max{u + 1}"] if u + 1 < len(units) else []) + (["sso0", "on0"] if u == 5 else [])]
            + ["sso1", "on1", "oT0", "oT1"])
        att_pool = signals("att_pool", ["ro0", "ro1"])
        xa_pe = signals("xa_pe", ["hqT0", "S0", "S1", "hqT1"] + [
            e for u in units for e in
            [f"pT{u}"] + ([f"oT{u - 1}"] if u else []) + ([f"S{u + 2}"] if u + 2 < 8 else []) + [f"pv{u}"]]
            + ["oT7"])
        xa_act = signals("xa_act", ["hq0", "hqT0", "hq1", "exp0", "hqT1"] + [
            e for u in units for e in
            ([f"exp{u + 1}"] if u < 7 else []) + [f"pT{u}"] + ([f"oT{u - 1}"] if u else []) + [f"o{u}"]]
            + ["oT7"])
        xa_dve = signals("xa_dve", ["max0"] + [
            e for u in units for e in
            ([f"max{u + 1}"] if u < 7 else []) + [f"rden{u}"] + ([f"oT{u - 1}"] if u else [])] + ["oT7"])

        SCALE = DK ** -0.5
        XSCALE = XD ** -0.5
        SLOPES = [2.0 ** (-8.0 * (h + 1) / HEADS) for h in range(HEADS)]
        USES = [len(range(s, NB, SLOTS)) for s in range(SLOTS)]

        def gain(norm, k):
            c = C_GAIN + 8 * NORMS.index(norm) + k
            return par[:, c:c + 1]

        def col(c):
            return par[:, c:c + 1]

        def tok(t):
            return slice(t * P, (t + 1) * P)

        block = ctx.enter_context(nc.Block())

        @block.sync
        def _(sp):
            def load(l, i, j=0):
                sp.dma_start(w_raw[:, i % SLOTS, :],
                             w_d[bass.ds(l * NB + j * SLOTS + i, 1)].rearrange("a p n -> (a p) n")
                             ).then_inc(w_in[i % SLOTS], 16)

            with sp.Fori(0, L) as l:
                sp.wait_ge(s_lo, FIRST + l * NB)
                load(l, 0)
                sp.dma_start(par[:, :], par_d[bass.ds(l, 1)].rearrange("a p n -> (a p) n")).then_inc(s_par, 16)
                load(l, 1)
                load(l, 2)
                sp.dma_start(m_raw, memT_d).then_inc(s_mraw, 16)
                with sp.Fori(0, NB // SLOTS - 1) as j:
                    for i in range(SLOTS, 2 * SLOTS):
                        sp.wait_ge(s_lo, FIRST + l * NB + j * SLOTS + i - SLOTS + 1)
                        load(l, i, j)
                for i in range(NB // SLOTS * SLOTS, NB):
                    sp.wait_ge(s_lo, FIRST + l * NB + i - SLOTS + 1)
                    load(l, i)
            sp.wait_ge(s_fin, TT)
            sp.dma_start(out_d.rearrange("(t p) n -> p t n", p=P), y[:, :, :]).then_inc(s_out, 16)
            sp.wait_ge(s_out, 16)

        @block.gpsimd
        def _(pool):
            def rsqrt(out, sum_sq, v, scale, n):
                nc.gpsimd.tensor_tensor(v, sum_sq, scale[:, 0:n], ALU.mult)
                pool.drain()
                nc.gpsimd.tensor_scalar(v, v, EPS, None, ALU.add)
                pool.drain()
                return nc.gpsimd.tensor_tensor(out, v, half[:, 0:n], ALU.pow)

            nc.gpsimd.memset(half[:, :], -0.5)
            nc.gpsimd.memset(over_d[:, :], 1.0 / D)
            nc.gpsimd.memset(over_dv[:, :], 1.0 / DV)
            nc.gpsimd.memset(zeros[:, :], 0.0)
            nc.gpsimd.memset(u_pad[:, :, :], 0.0)
            nc.gpsimd.memset(s_pad[:, :, :], 0.0)
            nc.gpsimd.memset(eps[:, :], EPS).then_inc(s_init, 1)
            pool.drain()
            pool.wait_ge(s_ssm, 1)
            rsqrt(rmem[:, :], ssm[:, :], var[:, :], over_d, TT).then_inc(s_rmem, 1)

            def norm(l, phase):
                pool.wait_ge(s_ssq, l * 4 + phase + 1)
                last = rsqrt(rinv[:, :], ssq[:, :], var[:, :], over_d, TT)
                if phase == 1:
                    pool.drain()
                    last = nc.gpsimd.tensor_scalar(nrinv[:, :], rinv[:, :], -1.0, None, ALU.mult)
                last.then_inc(s_rinv, 1)

            with pool.Fori(0, L) as l:
                norm(l, 0)
                norm(l, 1)
                for t in range(TT):
                    pool.wait_ge(att_dve.sem, att_dve.at(l, f"sso{t}"))
                    rsqrt(ro[:, t, :], sso[:, t, :], varo[:, t, :], over_dv, HEADS
                          ).then_inc(att_pool.sem, att_pool.one(f"ro{t}"))
                norm(l, 2)
                norm(l, 3)
            pool.wait_ge(s_ssq, 4 * L + 1)
            rsqrt(rinv[:, :], ssq[:, :], var[:, :], over_d, TT).then_inc(s_rinv, 1)

        @block.scalar
        def _(act):
            A = nc.scalar.activation

            def split(l, i, j=0, static=None):
                if i >= SLOTS:
                    act.wait_ge(s_blk, FIRST + l * NB + 2 * SLOTS * j + i - SLOTS + 1)
                else:
                    act.wait_ge(s_blk, FIRST + l * NB)
                s = i % SLOTS
                act.wait_ge(w_in[s], 16 * (l * USES[s] + 2 * j + i // SLOTS + 1))
                A(w_hi[:, s, :], w_raw[:, s, :], ACT.Copy).then_inc(s_hi, 1)

            def norm_start(l, phase):
                for k in range(KD):
                    if k % 2 == 0:
                        act.wait_ge(s_xT, l * 16 + phase * 4 + k // 2 + 1)
                    A(a_hi[:, k, :], DB[k // 2][:, (k % 2) * T:(k % 2 + 1) * T], ACT.Copy,
                      scale=gain(NORMS[phase], k)).then_inc(s_ahi, 1)

            def squares(l, phase):
                for t in range(TT):
                    act.drain()
                    if t == 0:
                        act.wait_ge(s_xup, FIRST + l * 16 + phase * 4)
                    last = A(junk[:, :], x[:, t, :], ACT.Square, accum_out=ssq[:, t:t + 1])
                last.then_inc(s_ssq, 1)

            def silu(l, f, j, c):
                act.wait_ge(s_blk, FIRST + l * NB + (B_FFN1, B_FFN2)[f] + 6 * j + (3 * c + 1 if c else 2))
                for t in range(TT):
                    A(sg[:, t, :], G[2 * (c % 2) + t][:, 0:CF], ACT.Silu, scale=rinv[:, t:t + 1]
                      ).then_inc(s_silu, 1)

            def hidden_hi(l, f, j, c):
                act.wait_ge(s_hT, l * 2 * STEPS + f * STEPS + 2 * j + c + 1)
                A(hT_hi[:, :, :], G[2 * (c % 2)][:, :].rearrange("p (k t) -> p k t", k=2), ACT.Copy
                  ).then_inc(s_hhi, 1)

            def ffn(l, f):
                base = (B_FFN1, B_FFN2)[f]
                norm_start(l, 3 * f)
                split(l, base + 2)
                squares(l, 3 * f)
                act.wait_ge(s_rinv, l * 4 + 3 * f + 1)
                silu(l, f, 0, 0)
                with act.Fori(0, (STEPS - 1) // 2) as j:
                    for c in (1, 2):
                        n = base + 3 * c
                        split(l, n, j)
                        split(l, n + 1, j)
                        hidden_hi(l, f, j, c - 1)
                        split(l, n + 2, j)
                        silu(l, f, j, c)
                j = (STEPS - 1) // 2
                for i in (base + FFN_BLOCKS, base + FFN_BLOCKS + 1):
                    if i < NB:
                        split(l, i)
                hidden_hi(l, f, j, 0)

            def copy_banks(banks, out_of, n):
                for b, bank in enumerate(banks):
                    last = A(out_of(b), bank[:, 0:n], ACT.Copy)
                return last

            def mixer(l):
                norm_start(l, 1)
                split(l, B_IN + 2)
                squares(l, 1)
                split(l, B_IN + 3)
                act.wait_ge(att_dve.sem, att_dve.at(l, "lam2"))
                A(elam[:, :], lam2[:, :], ACT.Exp).then_inc(att_act.sem, att_act.one("elam"))
                act.wait_ge(s_rinv, l * 4 + 2)
                act.wait_ge(s_blk, FIRST + l * NB + B_IN + 2)
                for t in range(TT):
                    last = A(sig[:, t, :], G[t][:, CC:2 * CC], ACT.Exp, scale=nrinv[:, t:t + 1])
                last.then_inc(conv_act.sem, conv_act.one("ecg"))
                split(l, B_IN + 4)
                act.wait_ge(conv_pe.sem, conv_pe.at(l, "uT"))
                A(u_pad[:, :, KC - 1:], DB[0][:, :].rearrange("p (c t) -> p c t", c=2), ACT.Copy
                  ).then_inc(conv_act.sem, conv_act.one("uT"))
                split(l, B_IN + 5)
                act.wait_ge(s_blk, FIRST + l * NB + B_IN + 4)
                for t in range(TT):
                    last = A(gbc[:, t, :], G[2 + t][:, :], ACT.Copy, scale=rinv[:, t:t + 1])
                last.then_inc(conv_act.sem, conv_act.one("gbc"))
                split(l, B_IN + 6)
                act.wait_ge(s_mraw, 16 * l + 16)
                for k in range(KD):
                    last = A(m_hi[:, k, :], m_raw[:, k, :], ACT.Copy, scale=gain("mem_norm", k))
                last.then_inc(mm_.sem, 1)
                split(l, B_IN + 7)
                act.wait_ge(conv_pe.sem, conv_pe.at(l, "sT"))
                A(s_pad[:, :, KS - 1:], DB[1][:, :].rearrange("p (c t) -> p c t", c=2), ACT.Copy
                  ).then_inc(conv_act.sem, conv_act.one("sT"))
                act.wait_ge(conv_pe.sem, conv_pe.at(l, "gbT"))
                A(gbT[:, :, :], DB[2][:, :].rearrange("p (c t) -> p c t", c=2), ACT.Copy
                  ).then_inc(conv_act.sem, conv_act.one("gbT"))
                split(l, B_IN + 8)
                for w, name in enumerate("qk"):
                    act.wait_ge(s_blk, FIRST + l * NB + B_IN + 7 + 2 * w)
                    for t in range(TT):
                        last = A(zqk[:, w, t, :], G[2 * (1 - w) + t][:, :], ACT.Copy, scale=rinv[:, t:t + 1])
                    last.then_inc(att_act.sem, att_act.one(name))
                    split(l, B_IN + 9 + 2 * w)
                    for b in range(2):
                        act.wait_ge(att_pe.sem, att_pe.at(l, f"{name}T{b}"))
                        last = A(qkT[:, 4 * w + 2 * b:4 * w + 2 * b + 2, :],
                                 DB[(3, 0, 1, 2)[2 * w + b]][:, :].rearrange("p (h t) -> p h t", h=2), ACT.Copy)
                    last.then_inc(att_act.sem, att_act.one(f"{name}T"))
                    split(l, B_IN + 10 + 2 * w)
                act.wait_ge(s_blk, FIRST + l * NB + B_IN + 11)
                for t in range(TT):
                    last = A(v_sb[:, t, :], G[2 + t][:, :], ACT.Copy, scale=rinv[:, t:t + 1])
                last.then_inc(att_act.sem, att_act.one("v"))
                split(l, B_KV + 2)

                def exp(u):
                    W = P * (u // HEADS + 1)
                    act.wait_ge(att_dve.sem, att_dve.at(l, f"max{u}"))
                    for c in range(2):
                        last = A(e_sb[:, u % 2, c, 0:W], s_sb[:, c, 0:W], ACT.Exp, scale=SCALE,
                                 bias=nmx[:, u % 2, c:c + 1], accum_out=den[:, u % 2, c:c + 1])
                    last.then_inc(att_act.sem, att_act.one(f"exp{u}"))

                def o_copy(t):
                    act.wait_ge(att_pe.sem, att_pe.at(l, f"pv{HEADS * t + HEADS - 1}"))
                    if t:
                        act.wait_ge(att_dve.sem, att_dve.at(l, "on0"))
                    A(o_sb[:, :, :], G[3][:, :].rearrange("p (h d) -> p h d", h=HEADS), ACT.Copy
                      ).then_inc(att_act.sem, att_act.one(f"o{t}"))

                exp(0)
                for u in units:
                    n = B_KV + u
                    if u + 1 < len(units):
                        exp(u + 1)
                    act.wait_ge(att_pe.sem, att_pe.at(l, f"aT{u}"))
                    kt = u // HEADS + 1
                    A(probT[:, 0:kt, :], G[2][:, 0:kt * P].rearrange("p (k t) -> p k t", k=kt), ACT.Copy
                      ).then_inc(att_act.sem, att_act.one(f"aT{u}"))
                    if u == 4:
                        o_copy(0)
                    if u % 2:
                        act.wait_ge(s_blk, FIRST + l * NB + n + 1)
                        ch = u // 2
                        for t in range(TT):
                            last = A((kx, vx)[ch // 2][:, t, (ch % 2) * N:(ch % 2 + 1) * N], G[t][:, :],
                                     ACT.Copy, scale=rmem[:, t:t + 1])
                        last.then_inc(att_act.sem, att_act.one(f"kv{ch}"))
                    split(l, n + 3)
                    if u == 3:
                        act.wait_ge(conv_pe.sem, conv_pe.at(l, "var"))
                        A(rstd[:, :], DB[3][:, 0:T], ACT.Sqrt, bias=eps[:, 0:1]
                          ).then_inc(conv_act.sem, conv_act.one("std"))
                    if u == 4:
                        act.wait_ge(conv_dve.sem, conv_dve.at(l, "norm"))
                        A(sq[:, :, :], acc[:, :, :], ACT.Exp, scale=-1.0
                          ).then_inc(conv_act.sem, conv_act.one("esilu"))
                    if u == 5:
                        act.wait_ge(conv_dve.sem, conv_dve.at(l, "cc"))
                        A(a_hi[:, 4:6, :], acc[:, :, :], ACT.Copy).then_inc(conv_act.sem, conv_act.one("cchi"))
                    if u == 6:
                        act.wait_ge(conv_dve.sem, conv_dve.at(l, "sc"))
                        A(a_hi[:, 6:8, :], accs[:, :, :], ACT.Copy).then_inc(conv_act.sem, conv_act.one("schi"))
                o_copy(1)

                def kx_copy(ch):
                    act.wait_ge(att_pe.sem, att_pe.at(l, f"kx{ch}"))
                    for b in range(2):
                        last = A(kxT[:, 4 * ch + 2 * b:4 * ch + 2 * b + 2, :],
                                 G[b][:, :].rearrange("p (h t) -> p h t", h=2), ACT.Copy)
                    last.then_inc(att_act.sem, att_act.one(f"kx{ch}"))

                def o_hi(t):
                    act.wait_ge(att_pe.sem, att_pe.at(l, f"oT{t}"))
                    A(a_hi[:, 0:4, tok(t)], G[2 + t][:, :].rearrange("p (h t) -> p h t", h=HEADS), ACT.Copy,
                      scale=gsub[:, 0:1]).then_inc(att_act.sem, att_act.one(f"oT{t}"))

                kx_copy(0)
                o_hi(0)
                split(l, B_OUT + 3)
                o_hi(1)
                split(l, B_Q)
                kx_copy(1)
                split(l, B_Q + 1)

            def cross(l):
                norm_start(l, 2)
                split(l, B_Q + 2)
                squares(l, 2)
                split(l, B_Q + 3)
                act.wait_ge(s_rinv, l * 4 + 3)

                def hq_copy(ch):
                    act.wait_ge(s_blk, FIRST + l * NB + B_Q + 2 * ch + 2)
                    for t in range(TT):
                        last = A(hq[:, t, ch * N:(ch + 1) * N], G[2 * ch + t][:, :], ACT.Copy,
                                 scale=rinv[:, t:t + 1])
                    last.then_inc(xa_act.sem, xa_act.one(f"hq{ch}"))

                def hqT_copy(ch):
                    act.wait_ge(xa_pe.sem, xa_pe.at(l, f"hqT{ch}"))
                    for b in range(2):
                        last = A(hqT[:, 4 * ch + 2 * b:4 * ch + 2 * b + 2, :],
                                 DB[2 * ch + b][:, :].rearrange("p (h t) -> p h t", h=2), ACT.Copy)
                    last.then_inc(xa_act.sem, xa_act.one(f"hqT{ch}"))

                def exp(u):
                    act.wait_ge(xa_dve.sem, xa_dve.at(l, f"max{u}"))
                    A(e_x[:, u % 2, :], G[u % 2][:, 0:T], ACT.Exp, scale=XSCALE, bias=nmx[:, u % 2, 0:1],
                      accum_out=den[:, u % 2, 0:1]).then_inc(xa_act.sem, xa_act.one(f"exp{u}"))

                def oT_hi(u):
                    h, t = u // 2, u % 2
                    act.wait_ge(xa_pe.sem, xa_pe.at(l, f"oT{u}"))
                    A(a_hi[:, 2 * h:2 * h + 2, tok(t)], G[3][:, T:2 * T].rearrange("p (k t) -> p k t", k=2),
                      ACT.Copy).then_inc(xa_act.sem, xa_act.one(f"oT{u}"))

                hq_copy(0)
                split(l, B_O)
                hqT_copy(0)
                split(l, B_O + 1)
                hq_copy(1)
                exp(0)
                hqT_copy(1)
                split(l, B_O + 2)
                for u in units:
                    if u < 7:
                        exp(u + 1)
                    act.wait_ge(xa_pe.sem, xa_pe.at(l, f"pT{u}"))
                    A(probT[:, :, :], G[2][:, 0:T].rearrange("p (k t) -> p k t", k=2), ACT.Copy
                      ).then_inc(xa_act.sem, xa_act.one(f"pT{u}"))
                    if u:
                        oT_hi(u - 1)
                    if u in (3, 5, 7):
                        split(l, B_O + 3 + (u - 3) // 2)
                    act.wait_ge(xa_pe.sem, xa_pe.at(l, f"pv{u}"))
                    act.wait_ge(xa_dve.sem, xa_dve.at(l, f"rden{u}"))
                    A(o_x[:, u % 2, :], G[3][:, 0:T], ACT.Copy, scale=rden[:, u % 2:u % 2 + 1]
                      ).then_inc(xa_act.sem, xa_act.one(f"o{u}"))
                oT_hi(7)

            act.dma_start(x[:, :, :], x_d.rearrange("(t p) n -> p t n", p=P)).then_inc(s_x, 16)
            act.dma_start(const[:, :], const_d).then_inc(s_const, 16)
            act.dma_start(vx[:, :, :], mem_d.rearrange("(t p) n -> p t n", p=P)).then_inc(s_mem, 16)
            act.wait_ge(s_mem, 16)
            for t in range(TT):
                act.drain()
                last = A(junk[:, :], vx[:, t, :], ACT.Square, accum_out=ssm[:, t:t + 1])
            last.then_inc(s_ssm, 1)
            act.wait_ge(s_init, 1)
            act.wait_ge(s_rmem, 1)
            act.wait_ge(s_x, 16)
            with act.Fori(0, L) as l:
                act.wait_ge(s_par, 16 * l + 16)
                split(l, 0)
                split(l, 1)
                ffn(l, 0)
                mixer(l)
                cross(l)
                ffn(l, 1)
            act.dma_start(fing, fin_d).then_inc(s_fing, 16)
            squares(L, 0)

        @block.vector
        def _(dve):
            V = nc.vector

            def split(l, i, j=0):
                dve.wait_ge(s_hi, l * NB + 2 * SLOTS * j + i + 1)
                s = i % SLOTS
                V.tensor_tensor(w_lo[:, s, :], w_raw[:, s, :], w_hi[:, s, :].bitcast(F32), ALU.subtract
                                ).then_inc(s_lo, 1)

            def norm_start(l, phase):
                for k in range(KD):
                    if k % 2 == 0:
                        dve.wait_ge(s_ahi, l * 32 + phase * 8 + k + 2)
                    V.scalar_tensor_tensor(a_lo[:, k, :], DB[k // 2][:, (k % 2) * T:(k % 2 + 1) * T],
                                           gain(NORMS[phase], k), a_hi[:, k, :].bitcast(F32),
                                           ALU.mult, ALU.subtract).then_inc(s_alo, 1)

            def x_update(l, phase, last_block, factor):
                dve.wait_ge(s_blk, FIRST + l * NB + last_block + 1)
                for n in range(2):
                    for t in range(TT):
                        xs = x[:, t, n * N:(n + 1) * N]
                        V.scalar_tensor_tensor(xs, DB[2 * n + t][:, :], factor, xs, ALU.mult, ALU.add
                                               ).then_inc(s_xup, 1)

            def hidden(l, f, j, c):
                dve.wait_ge(s_rinv, l * 4 + 3 * f + 1)
                for t in range(TT):
                    dve.wait_ge(s_silu, l * 4 * STEPS + f * 2 * STEPS + 4 * j + 2 * c + t + 1)
                    V.scalar_tensor_tensor(h_sb[:, t, :], G[2 * (c % 2) + t][:, CF:2 * CF], rinv[:, t:t + 1],
                                           sg[:, t, :], ALU.mult, ALU.mult).then_inc(s_h, 1)

            def hidden_lo(l, f, j, c):
                dve.wait_ge(s_hhi, l * 2 * STEPS + f * STEPS + 2 * j + c + 1)
                V.tensor_tensor(hT_lo[:, :, :], G[2 * (c % 2)][:, :].rearrange("p (k t) -> p k t", k=2),
                                hT_hi[:, :, :].bitcast(F32), ALU.subtract).then_inc(s_hlo, 1)

            def ffn(l, f):
                base = (B_FFN1, B_FFN2)[f]
                norm_start(l, 3 * f)
                split(l, base + 2)
                hidden(l, f, 0, 0)
                with dve.Fori(0, (STEPS - 1) // 2) as j:
                    for c in (1, 2):
                        n = base + 3 * c
                        split(l, n, j)
                        split(l, n + 1, j)
                        hidden_lo(l, f, j, c - 1)
                        split(l, n + 2, j)
                        hidden(l, f, j, c)
                j = (STEPS - 1) // 2
                for i in (base + FFN_BLOCKS, base + FFN_BLOCKS + 1):
                    if i < NB:
                        split(l, i)
                hidden_lo(l, f, j, 0)
                x_update(l, 3 * f, base + FFN_BLOCKS - 1, 0.5)

            def mixer(l):
                norm_start(l, 1)
                split(l, B_IN + 2)
                for i in range(2):
                    q, k = C_LAM + 2 * i * DK, C_LAM + (2 * i + 1) * DK
                    last = V.scalar_tensor_tensor(lamj[:, i, :], par[:, q:q + DK], 1.0, par[:, k:k + DK],
                                                  ALU.mult, ALU.mult, accum_out=lam2[:, i:i + 1])
                last.then_inc(att_dve.sem, att_dve.one("lam2"))
                V.tensor_scalar(gsub[:, :], col(C_SUB), col(C_REST), None, ALU.mult)
                split(l, B_IN + 3)
                dve.wait_ge(att_act.sem, att_act.at(l, "elam"))
                V.scalar_tensor_tensor(lam[:, :], elam[:, 0:1], col(C_INIT), elam[:, 1:2], ALU.add, ALU.subtract
                                       ).then_inc(att_dve.sem, att_dve.one("lam"))
                dve.wait_ge(s_rinv, l * 4 + 2)
                dve.wait_ge(conv_act.sem, conv_act.at(l, "ecg"))
                V.tensor_scalar(sig[:, :, :], sig[:, :, :], 1.0, None, ALU.add)
                dve.drain()
                V.reciprocal(sig[:, :, :], sig[:, :, :])
                dve.drain()
                for t in range(TT):
                    last = V.scalar_tensor_tensor(u_sb[:, t, :], G[t][:, 0:CC], rinv[:, t:t + 1], sig[:, t, :],
                                                  ALU.mult, ALU.mult)
                last.then_inc(conv_dve.sem, conv_dve.one("u"))
                split(l, B_IN + 4)

                def taps(ks):
                    for j in ks:
                        for c in range(2):
                            w = col(C_CCW + c * KC + j)
                            src = u_pad[:, c, j:j + T]
                            if j == 0:
                                V.tensor_scalar(acc[:, c, :], src, w, col(C_CCB + c), ALU.mult, ALU.add)
                            else:
                                last = V.scalar_tensor_tensor(acc[:, c, :], src, w, acc[:, c, :], ALU.mult, ALU.add)
                        if j == KC - 1:
                            last.then_inc(conv_dve.sem, conv_dve.one("acc"))
                        dve.drain()

                split(l, B_IN + 5)
                dve.wait_ge(conv_act.sem, conv_act.at(l, "uT"))
                taps(range(0, 5))
                split(l, B_IN + 6)
                dve.wait_ge(conv_act.sem, conv_act.at(l, "gbc"))
                dve.wait_ge(s_blk, FIRST + l * NB + B_IN + 5)
                for t in range(TT):
                    last = V.scalar_tensor_tensor(gch[:, t, :], G[t][:, 0:CC], rinv[:, t:t + 1],
                                                  gbc[:, t, CC:2 * CC], ALU.mult, ALU.mult)
                last.then_inc(conv_dve.sem, conv_dve.one("gch"))
                dve.wait_ge(mm_.sem, mm_.at(l, "hi"))
                for k in range(KD):
                    last = V.scalar_tensor_tensor(m_lo[:, k, :], m_raw[:, k, :], gain("mem_norm", k),
                                                  m_hi[:, k, :].bitcast(F32), ALU.mult, ALU.subtract)
                last.then_inc(mm_.sem, 1)
                split(l, B_IN + 7)
                taps(range(5, 10))
                split(l, B_IN + 8)
                taps(range(10, 15))
                split(l, B_IN + 9)
                taps(range(15, 20))
                split(l, B_IN + 10)
                taps(range(20, 25))
                split(l, B_KV)
                taps(range(25, 29))
                split(l, B_KV + 1)
                taps(range(29, 31))

                def scores(u):
                    t, h = u // HEADS, u % HEADS
                    W = P * (t + 1)
                    dve.wait_ge(att_pe.sem, att_pe.at(l, f"S{u}"))
                    if u:
                        dve.wait_ge(att_act.sem, att_act.at(l, f"exp{u - 1}"))
                    dist = const[:, K_DIST + t * T:K_DIST + t * T + W]
                    for c in range(2):
                        V.scalar_tensor_tensor(s_sb[:, c, 0:W], dist, -SLOPES[h] / SCALE, DB[c][:, 0:W],
                                               ALU.mult, ALU.add)
                    dve.drain()
                    V.reduce_max(mx[:, :], s_sb[:, :, 0:W], AX_X)
                    dve.drain()
                    V.tensor_scalar(nmx[:, u % 2, :], mx[:, :], -SCALE, None, ALU.mult
                                    ).then_inc(att_dve.sem, att_dve.one(f"max{u}"))

                def combine(u):
                    W = P * (u // HEADS + 1)
                    dve.wait_ge(att_act.sem, att_act.at(l, f"exp{u}"))
                    V.reciprocal(rden[:, :], den[:, u % 2, :])
                    dve.drain()
                    V.tensor_scalar(rden[:, 1:2], rden[:, 1:2], lam[:, 0:1], None, ALU.mult)
                    dve.drain()
                    V.tensor_scalar(e_sb[:, u % 2, 1, 0:W], e_sb[:, u % 2, 1, 0:W], rden[:, 1:2], None, ALU.mult)
                    dve.drain()
                    if u:
                        dve.wait_ge(att_pe.sem, att_pe.at(l, f"aT{u - 1}"))
                    V.scalar_tensor_tensor(prob[:, 0:W], e_sb[:, u % 2, 0, 0:W], rden[:, 0:1],
                                           e_sb[:, u % 2, 1, 0:W], ALU.mult, ALU.subtract
                                           ).then_inc(att_dve.sem, att_dve.one(f"a{u}"))

                def o_norm(t):
                    dve.wait_ge(att_act.sem, att_act.at(l, f"o{t}"))
                    for h in range(HEADS):
                        last = V.scalar_tensor_tensor(on_sb[:, t, h, :], o_sb[:, h, :], 1.0, o_sb[:, h, :],
                                                      ALU.mult, ALU.mult, accum_out=sso[:, t, h:h + 1])
                    last.then_inc(att_dve.sem, att_dve.one(f"sso{t}"))
                    dve.wait_ge(att_pool.sem, att_pool.at(l, f"ro{t}"))
                    for h in range(HEADS):
                        last = V.tensor_scalar(on_sb[:, t, h, :], o_sb[:, h, :], ro[:, t, h:h + 1], None, ALU.mult)
                    last.then_inc(att_dve.sem, att_dve.one(f"on{t}"))

                scores(0)
                split(l, B_KV + 2)
                for u in units:
                    combine(u)
                    if u + 1 < len(units):
                        scores(u + 1)
                    if u == 1:
                        dve.wait_ge(conv_pe.sem, conv_pe.at(l, "mean"))
                        for c in range(2):
                            V.tensor_tensor(acc[:, c, :], acc[:, c, :], DB[2][:, 0:T], ALU.subtract)
                        dve.drain()
                        V.tensor_tensor(sq[:, :, :], acc[:, :, :], acc[:, :, :], ALU.mult
                                        ).then_inc(conv_dve.sem, conv_dve.one("sq"))
                    if u == 4:
                        dve.wait_ge(conv_act.sem, conv_act.at(l, "std"))
                        V.reciprocal(rstd[:, :], rstd[:, :])
                        dve.drain()
                        for c in range(2):
                            V.tensor_tensor(acc[:, c, :], acc[:, c, :], rstd[:, :], ALU.mult)
                        dve.drain()
                        for c in range(2):
                            last = V.tensor_scalar(acc[:, c, :], acc[:, c, :], col(C_LNG + c), col(C_LNB + c),
                                                   ALU.mult, ALU.add)
                        last.then_inc(conv_dve.sem, conv_dve.one("norm"))
                    if u == 5:
                        o_norm(0)
                        dve.wait_ge(conv_act.sem, conv_act.at(l, "esilu"))
                        V.tensor_scalar(sq[:, :, :], sq[:, :, :], 1.0, None, ALU.add)
                        dve.drain()
                        V.reciprocal(sq[:, :, :], sq[:, :, :])
                        dve.drain()
                        V.tensor_tensor(acc[:, :, :], acc[:, :, :], sq[:, :, :], ALU.mult
                                        ).then_inc(conv_dve.sem, conv_dve.one("cc"))
                    if u == 6:
                        dve.wait_ge(conv_act.sem, conv_act.at(l, "cchi"))
                        V.tensor_tensor(a_lo[:, 4:6, :], acc[:, :, :], a_hi[:, 4:6, :].bitcast(F32), ALU.subtract
                                        ).then_inc(conv_dve.sem, conv_dve.one("cclo"))
                        dve.wait_ge(conv_act.sem, conv_act.at(l, "gbT"))
                        for j in range(KS):
                            for c in range(2):
                                w = col(C_SCW + c * KS + j)
                                src = s_pad[:, c, j:j + T]
                                if j == 0:
                                    V.tensor_scalar(accs[:, c, :], src, w, None, ALU.mult)
                                else:
                                    V.scalar_tensor_tensor(accs[:, c, :], src, w, accs[:, c, :], ALU.mult, ALU.add)
                            dve.drain()
                        V.tensor_tensor(accs[:, :, :], accs[:, :, :], gbT[:, :, :], ALU.mult
                                        ).then_inc(conv_dve.sem, conv_dve.one("sc"))
                    split(l, B_KV + u + 3)
                dve.wait_ge(conv_act.sem, conv_act.at(l, "schi"))
                V.tensor_tensor(a_lo[:, 6:8, :], accs[:, :, :], a_hi[:, 6:8, :].bitcast(F32), ALU.subtract
                                ).then_inc(conv_dve.sem, conv_dve.one("sclo"))

                def o_lo(t):
                    dve.wait_ge(att_act.sem, att_act.at(l, f"oT{t}"))
                    V.scalar_tensor_tensor(a_lo[:, 0:4, tok(t)], G[2 + t][:, :].rearrange("p (h t) -> p h t", h=HEADS),
                                           gsub[:, 0:1], a_hi[:, 0:4, tok(t)].bitcast(F32), ALU.mult, ALU.subtract
                                           ).then_inc(att_dve.sem, att_dve.one(f"oT{t}"))

                o_norm(1)
                o_lo(0)
                split(l, B_OUT + 3)
                o_lo(1)
                split(l, B_Q)
                split(l, B_Q + 1)
                x_update(l, 1, B_OUT + 3, 1.0)

            def cross(l):
                norm_start(l, 2)
                split(l, B_Q + 2)
                split(l, B_Q + 3)
                split(l, B_O)
                split(l, B_O + 1)

                def row_max(u):
                    dve.wait_ge(xa_pe.sem, xa_pe.at(l, f"S{u}"))
                    V.reduce_max(mx[:, u % 2:u % 2 + 1], G[u % 2][:, 0:T], AX_X)
                    dve.drain()
                    V.tensor_scalar(nmx[:, u % 2, 0:1], mx[:, u % 2:u % 2 + 1], -XSCALE, None, ALU.mult
                                    ).then_inc(xa_dve.sem, xa_dve.one(f"max{u}"))

                def oT_lo(u):
                    h, t = u // 2, u % 2
                    dve.wait_ge(xa_act.sem, xa_act.at(l, f"oT{u}"))
                    V.tensor_tensor(a_lo[:, 2 * h:2 * h + 2, tok(t)],
                                    G[3][:, T:2 * T].rearrange("p (k t) -> p k t", k=2),
                                    a_hi[:, 2 * h:2 * h + 2, tok(t)].bitcast(F32), ALU.subtract
                                    ).then_inc(xa_dve.sem, xa_dve.one(f"oT{u}"))

                row_max(0)
                for u in units:
                    if u < 7:
                        row_max(u + 1)
                    dve.wait_ge(xa_act.sem, xa_act.at(l, f"exp{u}"))
                    V.reciprocal(rden[:, u % 2:u % 2 + 1], den[:, u % 2, 0:1]
                                 ).then_inc(xa_dve.sem, xa_dve.one(f"rden{u}"))
                    if u == 0:
                        split(l, B_O + 2)
                    if u:
                        oT_lo(u - 1)
                    if u in (3, 5, 7):
                        split(l, B_O + 3 + (u - 3) // 2)
                oT_lo(7)
                x_update(l, 2, B_O + 3, 1.0)

            lamj = v_sb[:, 0, 0:2 * DK].rearrange("p (a k) -> p a k", a=2)
            dve.sem_inc(s_lo, FIRST)
            dve.sem_inc(s_xup, FIRST)
            dve.wait_ge(s_init, 1)
            dve.wait_ge(s_const, 16)
            dve.wait_ge(s_x, 16)
            with dve.Fori(0, L) as l:
                dve.wait_ge(s_par, 16 * l + 16)
                split(l, 0)
                split(l, 1)
                ffn(l, 0)
                mixer(l)
                cross(l)
                ffn(l, 1)
            dve.wait_ge(s_fing, 16)
            dve.wait_ge(s_rinv, 4 * L + 1)
            for t in range(TT):
                V.scalar_tensor_tensor(y[:, t, :], x[:, t, :], rinv[:, t:t + 1], fing, ALU.mult, ALU.mult
                                       ).then_inc(s_fin, 1)

        @block.tensor
        def _(pe):
            M = nc.tensor.matmul
            TR = nc.tensor.transpose

            def weights(l, i, j=0):
                pe.wait_ge(s_lo, FIRST + l * NB + 2 * SLOTS * j + i + 1)
                return w_hi[:, i % SLOTS, :], w_lo[:, i % SLOTS, :]

            def product(out, hi, lo, whi, wlo, start, stop):
                M(out, hi, whi, start=start, stop=False)
                M(out, hi, wlo, start=False, stop=False)
                return M(out, lo, whi, start=False, stop=stop)

            def wide(l, i, ahi, alo, pair, ks, width=N, j=0, ready=None):
                whi, wlo = weights(l, i, j)
                for n, k in enumerate(ks):
                    if ready is not None:
                        pe.wait_ge(s_alo, ready + k + 1)
                    for t in range(TT):
                        last = product(G[2 * pair + t][:, 0:width], ahi[:, k, tok(t)], alo[:, k, tok(t)],
                                       whi[:, n * width:(n + 1) * width], wlo[:, n * width:(n + 1) * width],
                                       k == 0, k == KD - 1)
                last.then_inc(s_blk, 1)

            def down(l, i, hi, lo, ks, start, stop, j=0):
                whi, wlo = weights(l, i, j)
                for n, k in enumerate(ks):
                    for c in range(2):
                        w = slice(n * D + c * N, n * D + (c + 1) * N)
                        for t in range(TT):
                            last = product(DB[2 * c + t][:, :], hi[:, k, tok(t)], lo[:, k, tok(t)], whi[:, w],
                                           wlo[:, w], start and n == 0, stop and n == 1)
                last.then_inc(s_blk, 1)

            def x_transposes(l, phase):
                for b in range(4):
                    pe.wait_ge(s_xup, FIRST + l * 16 + (phase * 4 - 2 * (1 - b // 2) if phase else 0))
                    for kk in range(2):
                        for t in range(TT):
                            last = TR(DB[b][:, kk * T + t * P:kk * T + (t + 1) * P],
                                      x[:, t, (2 * b + kk) * P:(2 * b + kk + 1) * P], ident)
                    last.then_inc(s_xT, 1)

            def transpose_pairs(src, banks, signals_, names):
                for b, bank in enumerate(banks):
                    for i in range(2):
                        for t in range(TT):
                            last = TR(bank[:, i * T + t * P:i * T + (t + 1) * P], src(t, 2 * b + i), ident)
                    if names[b]:
                        last.then_inc(signals_.sem, signals_.one(names[b]))

            def ffn(l, f):
                base = (B_FFN1, B_FFN2)[f]
                x_transposes(l, 3 * f)
                ready = l * 32 + 3 * f * 8
                wide(l, base, a_hi, a_lo, 0, range(4), ready=ready)
                wide(l, base + 1, a_hi, a_lo, 0, range(4, 8), ready=ready)
                for b in range(4):
                    M(DB[b][:, :], zeros[:, 0:P], zeros[:, :], start=True, stop=False)

                def transposes(j, c):
                    pe.wait_ge(s_h, l * 4 * STEPS + f * 2 * STEPS + 4 * j + 2 * c + 2)
                    for k in range(2):
                        for t in range(TT):
                            last = TR(G[2 * (c % 2)][:, k * T + t * P:k * T + (t + 1) * P],
                                      h_sb[:, t, k * P:(k + 1) * P], ident)
                    last.then_inc(s_hT, 1)

                def hidden_ready(j, c):
                    pe.wait_ge(s_hlo, l * 2 * STEPS + f * STEPS + 2 * j + c + 1)

                with pe.Fori(0, (STEPS - 1) // 2) as j:
                    for c in (1, 2):
                        n = base + 3 * c
                        wide(l, n - 1, a_hi, a_lo, c % 2, range(4), j=j)
                        transposes(j, c - 1)
                        wide(l, n, a_hi, a_lo, c % 2, range(4, 8), j=j)
                        hidden_ready(j, c - 1)
                        down(l, n + 1, hT_hi, hT_lo, range(2), False, False, j=j)
                j = (STEPS - 1) // 2
                transposes(j, 0)
                hidden_ready(j, 0)
                down(l, base + FFN_BLOCKS - 1, hT_hi, hT_lo, range(2), False, True)

            def mixer(l):
                x_transposes(l, 1)
                ready = l * 32 + 8
                wide(l, B_IN, a_hi, a_lo, 0, range(4), ready=ready)
                wide(l, B_IN + 1, a_hi, a_lo, 0, range(4, 8), ready=ready)
                wide(l, B_IN + 2, a_hi, a_lo, 1, range(4))
                pe.wait_ge(conv_dve.sem, conv_dve.at(l, "u"))
                transpose_pairs(lambda t, i: u_sb[:, t, i * P:(i + 1) * P], [DB[0]], conv_pe, ["uT"])
                wide(l, B_IN + 3, a_hi, a_lo, 1, range(4, 8))
                wide(l, B_IN + 4, a_hi, a_lo, 0, range(8), width=CC)
                pe.wait_ge(conv_act.sem, conv_act.at(l, "gbc"))
                wide(l, B_IN + 5, a_hi, a_lo, 1, range(4))
                pe.wait_ge(conv_dve.sem, conv_dve.at(l, "gch"))
                transpose_pairs(lambda t, i: gch[:, t, i * P:(i + 1) * P], [DB[1]], conv_pe, ["sT"])
                transpose_pairs(lambda t, i: gbc[:, t, i * P:(i + 1) * P], [DB[2]], conv_pe, ["gbT"])
                wide(l, B_IN + 6, a_hi, a_lo, 1, range(4, 8))
                wide(l, B_IN + 7, a_hi, a_lo, 0, range(4))
                pe.wait_ge(att_act.sem, att_act.at(l, "q"))
                transpose_pairs(lambda t, i: zqk[:, 0, t, i * P:(i + 1) * P], [DB[3], DB[0]], att_pe, ["qT0", "qT1"])
                wide(l, B_IN + 8, a_hi, a_lo, 0, range(4, 8))
                wide(l, B_IN + 9, a_hi, a_lo, 1, range(4))
                pe.wait_ge(conv_act.sem, conv_act.at(l, "gbT"))
                pe.wait_ge(att_act.sem, att_act.at(l, "k"))
                transpose_pairs(lambda t, i: zqk[:, 1, t, i * P:(i + 1) * P], [DB[1], DB[2]], att_pe, ["kT0", "kT1"])
                wide(l, B_IN + 10, a_hi, a_lo, 1, range(4, 8))

                def S(u):
                    t, h = u // HEADS, u % HEADS
                    W = P * (t + 1)
                    if u:
                        pe.wait_ge(att_dve.sem, att_dve.at(l, f"max{u - 1}"))
                    for c in range(2):
                        r = slice(c * DK, (c + 1) * DK)
                        last = M(DB[c][:, 0:W], qkT[r, h, tok(t)], qkT[r, HEADS + h, 0:W], start=True, stop=True)
                    last.then_inc(att_pe.sem, att_pe.one(f"S{u}"))

                def aT(u):
                    pe.wait_ge(att_dve.sem, att_dve.at(l, f"a{u}"))
                    for k in range(u // HEADS + 1):
                        last = TR(G[2][:, k * P:(k + 1) * P], prob[:, k * P:(k + 1) * P], ident)
                    last.then_inc(att_pe.sem, att_pe.one(f"aT{u}"))

                def pv(u):
                    t, h = u // HEADS, u % HEADS
                    pe.wait_ge(att_act.sem, att_act.at(l, f"aT{u}"))
                    if u == HEADS:
                        pe.wait_ge(att_act.sem, att_act.at(l, "o0"))
                    for k in range(t + 1):
                        last = M(G[3][:, h * DV:(h + 1) * DV], probT[:, k, :], v_sb[:, k, h * DV:(h + 1) * DV],
                                 start=(k == 0), stop=(k == t))
                    last.then_inc(att_pe.sem, att_pe.one(f"pv{u}"))

                pe.wait_ge(att_act.sem, att_act.at(l, "kT"))
                S(0)
                pe.wait_ge(mm_.sem, mm_.at(l, "lo"))
                for u in units:
                    n = B_KV + u
                    if u % 2 == 0 and u:
                        pe.wait_ge(att_act.sem, att_act.at(l, f"kv{u // 2 - 1}"))
                    if u == 0:
                        S(1)
                    wide(l, n, m_hi, m_lo, 0, range(4 * (u % 2), 4 * (u % 2) + 4))
                    if u:
                        pv(u - 1)
                    if u == 0:
                        pe.wait_ge(att_act.sem, att_act.at(l, "v"))
                    aT(u)
                    if u + 2 < len(units):
                        S(u + 2)
                    if u == 1:
                        pe.wait_ge(conv_dve.sem, conv_dve.at(l, "acc"))
                        for c in range(2):
                            last = M(DB[2][:, 0:T], mean_w, acc[:, c, :], start=(c == 0), stop=(c == 1))
                        last.then_inc(conv_pe.sem, conv_pe.one("mean"))
                    if u == 3:
                        pe.wait_ge(conv_dve.sem, conv_dve.at(l, "sq"))
                        for c in range(2):
                            last = M(DB[3][:, 0:T], mean_w, sq[:, c, :], start=(c == 0), stop=(c == 1))
                        last.then_inc(conv_pe.sem, conv_pe.one("var"))

                def out(i):
                    k = 2 * OUT_ORDER[i]
                    down(l, B_OUT + i, a_hi, a_lo, (k, k + 1), i == 0, i == 3)

                def kx_transposes(ch):
                    transpose_pairs(lambda t, i: kx[:, t, (4 * ch + i) * P:(4 * ch + i + 1) * P], [G[0], G[1]],
                                    att_pe, [None, f"kx{ch}"])

                def o_transposes(t):
                    pe.wait_ge(att_dve.sem, att_dve.at(l, f"on{t}"))
                    for h in range(HEADS):
                        last = TR(G[2 + t][:, h * P:(h + 1) * P], on_sb[:, t, h, :], ident)
                    last.then_inc(att_pe.sem, att_pe.one(f"oT{t}"))

                pe.wait_ge(conv_dve.sem, conv_dve.at(l, "cclo"))
                out(0)
                pv(7)
                pe.wait_ge(att_act.sem, att_act.at(l, "kv3"))
                kx_transposes(0)
                o_transposes(0)
                pe.wait_ge(conv_dve.sem, conv_dve.at(l, "sclo"))
                out(1)
                o_transposes(1)
                pe.wait_ge(att_act.sem, att_act.at(l, "kx0"))
                kx_transposes(1)
                pe.wait_ge(att_dve.sem, att_dve.at(l, "oT1"))
                out(2)
                out(3)

            def cross(l):
                x_transposes(l, 2)
                ready = l * 32 + 16
                pe.wait_ge(att_act.sem, att_act.at(l, "kx1"))
                wide(l, B_Q, a_hi, a_lo, 0, range(4), ready=ready)
                wide(l, B_Q + 1, a_hi, a_lo, 0, range(4, 8), ready=ready)
                wide(l, B_Q + 2, a_hi, a_lo, 1, range(4))

                def hq_transposes(ch):
                    pe.wait_ge(xa_act.sem, xa_act.at(l, f"hq{ch}"))
                    transpose_pairs(lambda t, i: hq[:, t, (4 * ch + i) * P:(4 * ch + i + 1) * P],
                                    [DB[2 * ch], DB[2 * ch + 1]], xa_pe, [None, f"hqT{ch}"])

                def S(u):
                    h, t = u // 2, u % 2
                    if u == 0:
                        pe.wait_ge(xa_act.sem, xa_act.at(l, "hqT0"))
                    if u == 4:
                        pe.wait_ge(xa_act.sem, xa_act.at(l, "hqT1"))
                    for k in range(2):
                        last = M(G[u % 2][:, 0:T], hqT[:, 2 * h + k, tok(t)], kxT[:, 2 * h + k, :],
                                 start=(k == 0), stop=(k == 1))
                    last.then_inc(xa_pe.sem, xa_pe.one(f"S{u}"))

                def oT(u):
                    pe.wait_ge(xa_act.sem, xa_act.at(l, f"o{u}"))
                    for k in range(2):
                        last = TR(G[3][:, T + k * P:T + (k + 1) * P], o_x[:, u % 2, k * P:(k + 1) * P], ident)
                    last.then_inc(xa_pe.sem, xa_pe.one(f"oT{u}"))

                hq_transposes(0)
                wide(l, B_Q + 3, a_hi, a_lo, 1, range(4, 8))
                S(0)
                S(1)
                hq_transposes(1)
                for u in units:
                    h = u // 2
                    pe.wait_ge(xa_act.sem, xa_act.at(l, f"exp{u}"))
                    for k in range(2):
                        last = TR(G[2][:, k * P:(k + 1) * P], e_x[:, u % 2, k * P:(k + 1) * P], ident)
                    last.then_inc(xa_pe.sem, xa_pe.one(f"pT{u}"))
                    if u:
                        oT(u - 1)
                    if u + 2 < len(units):
                        S(u + 2)
                    if u in (3, 5, 7):
                        b = (u - 3) // 2
                        down(l, B_O + b, a_hi, a_lo, (2 * b, 2 * b + 1), b == 0, False)
                    pe.wait_ge(xa_act.sem, xa_act.at(l, f"pT{u}"))
                    if u:
                        pe.wait_ge(xa_dve.sem, xa_dve.at(l, f"oT{u - 1}"))
                    for k in range(2):
                        last = M(G[3][:, 0:XD], probT[:, k, :], vx[:, k, h * XD:(h + 1) * XD],
                                 start=(k == 0), stop=(k == 1))
                    last.then_inc(xa_pe.sem, xa_pe.one(f"pv{u}"))
                oT(7)
                pe.wait_ge(xa_dve.sem, xa_dve.at(l, "oT7"))
                down(l, B_O + 3, a_hi, a_lo, (6, 7), False, True)

            pe.sem_inc(s_blk, FIRST)
            pe.wait_ge(s_const, 16)
            pe.wait_ge(s_x, 16)
            pe.wait_ge(s_init, 1)
            with pe.Fori(0, L) as l:
                ffn(l, 0)
                mixer(l)
                cross(l)
                ffn(l, 1)


def kernel(**inputs):
    import numpy as np
    import concourse.bacc as bacc
    from concourse.bass_utils import run_bass_kernel_spmd

    a = {k: np.asarray(v) for k, v in inputs.items()}

    def chunks(w, cols):
        k = w.shape[0] // P
        return w.reshape(k, P, cols).transpose(1, 0, 2).reshape(P, k * cols)

    stream = np.empty((L * NB, P, BLOCK), np.float32)
    at = 0

    def put(w):
        nonlocal at
        stream[at] = chunks(w, w.shape[1])
        at += 1

    def put_wide(w):
        put(w[:D // 2])
        put(w[D // 2:])

    for l in range(L):
        def ffn(n):
            gate, up, down = (a[f"ffn{n}_w_{k}"][l] for k in ("gate", "up", "down"))
            for c in range(STEPS + 1):
                s = slice(c * CF, (c + 1) * CF)
                if c < STEPS:
                    put_wide(np.concatenate([gate[:, s], up[:, s]], 1))
                if c:
                    put(down[(c - 1) * CF:c * CF])

        ffn(1)
        w = a["w_in"][l]
        for c in (3 * N, 4 * N):
            put_wide(w[:, c:c + N])
        put(w[:, 5 * N:5 * N + CC])
        for c in (0, N, 2 * N):
            put_wide(w[:, c:c + N])
        for c in range(0, 2 * D, N):
            put_wide(a["xa_wkv"][l][:, c:c + N])
        for k in OUT_ORDER:
            put(a["w_out"][l][k * 2 * P:(k + 1) * 2 * P])
        for c in (0, N):
            put_wide(a["xa_wq"][l][:, c:c + N])
        for k in range(4):
            put(a["xa_wo"][l][k * 2 * P:(k + 1) * 2 * P])
        ffn(2)
    assert at == L * NB

    par = np.empty((L, P, NPAR), np.float32)
    for l in range(L):
        for n, name in enumerate(NORMS):
            par[l, :, C_GAIN + 8 * n:C_GAIN + 8 * n + 8] = a[name][l].reshape(8, P).T
        par[l, :, C_SUB] = a["diff_subln"][l]
        for c in range(2):
            ch = slice(c * P, (c + 1) * P)
            par[l, :, C_CCW + c * KC:C_CCW + (c + 1) * KC] = a["cc_dw"][l][:, ch].T
            par[l, :, C_CCB + c] = a["cc_dw_b"][l][ch]
            par[l, :, C_LNG + c] = a["cc_ln_g"][l][ch]
            par[l, :, C_LNB + c] = a["cc_ln_b"][l][ch]
            par[l, :, C_SCW + c * KS:C_SCW + (c + 1) * KS] = a["sc_dw"][l][:, ch].T
        for n, name in enumerate(("lam_q1", "lam_k1", "lam_q2", "lam_k2")):
            par[l, :, C_LAM + n * DK:C_LAM + (n + 1) * DK] = a[name][l]
        par[l, :, C_INIT] = 0.8 - 0.6 * float(np.exp(-0.3 * l))
        par[l, :, C_REST] = 1.0 - (0.8 - 0.6 * float(np.exp(-0.3 * l)))

    const = np.zeros((P, NCONST), np.float32)
    const[:, K_ID:K_ID + P] = np.eye(P)
    const[:, K_MEAN:K_MEAN + P] = 1.0 / CC
    for t in range(TT):
        dist = (t * P + np.arange(P))[:, None] - np.arange(T)[None, :]
        const[:, K_DIST + t * T:K_DIST + (t + 1) * T] = np.where(dist >= 0, dist, MASKED)

    arrays = {
        "x_dram": np.ascontiguousarray(a["x"].reshape(T, D)),
        "mem_dram": np.ascontiguousarray(a["mem"].reshape(T, D)),
        "memT_dram": np.ascontiguousarray(a["mem"].reshape(T, KD, P).transpose(2, 1, 0)),
        "w_dram": stream,
        "par_dram": par,
        "const_dram": const,
        "fin_dram": np.ascontiguousarray(np.broadcast_to(a["final_norm"][None, :], (P, D))),
    }
    nc = bacc.Bacc("TRN2", target_bir_lowering=False, num_devices=1)
    args = [nc.dram_tensor(k, v.shape, F32, kind="ExternalInput").ap() for k, v in arrays.items()]
    out = nc.dram_tensor("out_dram", (T, D), F32, kind="ExternalOutput").ap()
    hymba_kernel(nc, *args, out)
    r = run_bass_kernel_spmd(nc, [arrays], core_ids=[0])
    return r.results[0]["out_dram"].reshape(1, T, D)
```

```python
from contextlib import ExitStack

import concourse.bass as bass
from concourse import mybir

F32 = mybir.dt.float32
F32R = mybir.dt.float32r
BF16 = mybir.dt.bfloat16
ALU = mybir.AluOpType
ACT = mybir.ActivationFunctionType
AX_X = mybir.AxisListType.X

P = 128
EPS = 1e-6
NORMS = ("ffn1_norm", "mix_norm", "xa_norm", "ffn2_norm", "mem_norm")

D, T, L, F = 1024, 256, 2, 2816
HEADS, DK, DV = 4, 64, 128
CC, KC, KS = 256, 31, 3
XH, XD = 4, 256
KD = D // P
TT = T // P
N = 512
CF = N // 2
STEPS = F // CF
BLOCK = 2048
SLOTS = 3
FIRST = 1

FFN_BLOCKS = 3 * STEPS
B_FFN1 = 0
B_IN = B_FFN1 + FFN_BLOCKS
B_KV = B_IN + 11
B_OUT = B_KV + 8
B_Q = B_OUT + 4
B_O = B_Q + 4
B_FFN2 = B_O + 4
NB = B_FFN2 + FFN_BLOCKS
OUT_ORDER = (3, 2, 0, 1)
A_PAIR = (1, 0, 2, 3)
A_CC, A_SC, A_ATT = 0, 2, 4

C_GAIN = 0
C_SUB = C_GAIN + 8 * len(NORMS)
C_CCW = C_SUB + 1
C_CCB = C_CCW + 2 * KC
C_LNG = C_CCB + 2
C_LNB = C_LNG + 2
C_SCW = C_LNB + 2
C_LAM = C_SCW + 2 * KS
C_INIT = C_LAM + 4 * DK
C_REST = C_INIT + 1
NPAR = C_REST + 1

K_ID = 0
K_MEAN = K_ID + P
K_DIST = K_MEAN + P
NCONST = K_DIST + TT * T
MASKED = 1e38


class Signals:

    def __init__(self, sem, events):
        self.sem, self.order, self.n, self.next = sem, {e: i for i, e in enumerate(events)}, len(events), 0
        assert len(self.order) == self.n

    def one(self, event):
        assert self.order[event] == self.next % self.n, event
        self.next += 1
        return 1

    def at(self, layer, event):
        return layer * self.n + self.order[event] + 1


def hymba_kernel(nc, x_d, mem_d, memT_d, w_d, par_d, const_d, fin_d, out_d):
    ctx = ExitStack()
    with ctx:
        def sb(name, shape, dt=F32):
            return ctx.enter_context(nc.sbuf_tensor(name, shape, dt))

        def sem(name):
            return ctx.enter_context(nc.semaphore(name))

        def signals(name, events):
            return Signals(sem(name), events)

        w_raw = sb("w_raw", [P, SLOTS, BLOCK])
        w_hi = sb("w_hi", [P, SLOTS, BLOCK], F32R)
        w_lo = sb("w_lo", [P, SLOTS, BLOCK], F32R)
        x = sb("x", [P, TT, D])
        a_hi = sb("a_hi", [P, KD, T], F32R)
        a_lo = sb("a_lo", [P, KD, T], F32R)
        m_hi = sb("m_hi", [P, KD, T], F32R)
        m_lo = sb("m_lo", [P, KD, T], F32R)
        hT_hi = sb("hT_hi", [P, 2, T], F32R)
        hT_lo = sb("hT_lo", [P, 2, T], F32R)
        const = sb("const", [P, NCONST])
        ident = const[:, K_ID:K_ID + P]
        mean_w = const[:, K_MEAN:K_MEAN + P]
        par = sb("par", [P, NPAR])
        zeros = sb("zeros", [P, N], BF16)
        half = sb("half", [P, 8])
        over_d = sb("over_d", [P, 8])
        over_dv = sb("over_dv", [P, 8])
        eps = sb("eps", [P, 1])
        ssq = sb("ssq", [P, TT])
        var = sb("var", [P, TT])
        rinv = sb("rinv", [P, TT])
        nrinv = sb("nrinv", [P, TT])
        ssm = sb("ssm", [P, TT])
        rmem = sb("rmem", [P, TT])
        junk = sb("junk", [P, D], BF16)
        zqk = sb("zqk", [P, 2, TT, N])
        qkT = sb("qkT", [P, 2 * HEADS, T])
        hq = zqk[:, :, :, :].rearrange("p a t n -> p (a t n)").rearrange("p (t n) -> p t n", t=TT)
        hqT = qkT
        v_sb = sb("v_sb", [P, TT, N])
        u_sb = sb("u_sb", [P, TT, CC])
        gbc = sb("gbc", [P, TT, N])
        gch = sb("gch", [P, TT, CC])
        sig = sb("sig", [P, TT, CC])
        u_pad = sb("u_pad", [P, 2, KC - 1 + T])
        s_pad = sb("s_pad", [P, 2, KS - 1 + T])
        gbT = sb("gbT", [P, 2, T])
        acc = sb("acc", [P, 2, T])
        accs = sb("accs", [P, 2, T])
        sq = sb("sq", [P, 2, T])
        rstd = sb("rstd", [P, T])
        s_sb = sb("s_sb", [P, 2, T])
        e_sb = sb("e_sb", [P, 2, 2, T])
        prob = sb("prob", [P, T])
        probT = sb("probT", [P, 2, 2, P])
        o_sb = sb("o_sb", [P, HEADS, DV])
        on_sb = sb("on_sb", [P, TT, HEADS, DV])
        sg = sig
        h_sb = u_sb
        kx = sb("kx", [P, TT, D])
        m_raw = kx[:, :, :].rearrange("p t n -> p (t n)").rearrange("p (k m) -> p k m", k=KD)
        vx = sb("vx", [P, TT, D])
        kxT = sb("kxT", [P, KD, T])
        e_x = e_sb[:, :, 0, :]
        o_x = s_sb
        mx = sb("mx", [P, 2])
        nmx = sb("nmx", [P, 2, 2])
        den = sb("den", [P, 2, 2])
        rden = sb("rden", [P, 2])
        sso = sb("sso", [P, TT, HEADS])
        varo = sb("varo", [P, TT, HEADS])
        ro = sb("ro", [P, TT, HEADS])
        lam2 = sb("lam2", [P, 2])
        elam = sb("elam", [P, 2])
        lam = sb("lam", [P, 1])
        gsub = sb("gsub", [P, 1])
        fing = kxT[:, 0:4, :].rearrange("p k m -> p (k m)")
        y = vx

        G = [ctx.enter_context(nc.psum_tensor(f"G{i}", [P, N], F32)) for i in range(4)]
        DB = [ctx.enter_context(nc.psum_tensor(f"D{i}", [P, N], F32)) for i in range(4)]

        s_x = [sem("x_loaded0"), sem("x_loaded1")]
        s_const = sem("const_loaded")
        s_mem = sem("mem_loaded")
        s_fing = sem("final_gain_loaded")
        s_par = sem("params_loaded")
        s_mraw = sem("memT_loaded")
        s_out = sem("out_stored")
        w_in = [sem(f"w_loaded{i}") for i in range(SLOTS)]
        s_hi = sem("w_hi_ready")
        s_lo = sem("w_lo_ready")
        s_blk = sem("block_multiplied")
        s_init = sem("constants_set")
        s_rmem = sem("rmem_ready")
        s_ssm = sem("ssm_ready")
        s_xup = sem("x_updated")
        s_half = sem("first_half_summed")
        s_xT = sem("xT_in_psum")
        s_ahi = sem("a_hi_ready")
        s_alo = sem("a_lo_ready")
        s_ssq = sem("ssq_ready")
        s_rinv = sem("rinv_ready")
        s_silu = sem("silu_ready")
        s_h = sem("h_ready")
        s_hT = sem("hT_in_psum")
        s_hhi = sem("hT_hi_ready")
        s_hlo = sem("hT_lo_ready")
        s_fin = sem("final_ready")
        mm_ = signals("mem_ready", ["hi", "lo"])
        conv_pe = signals("conv_pe", ["uT", "sT", "gbT", "mean", "var"])
        conv_act = signals("conv_act", ["ecg", "uT", "gbc", "sT", "gbT", "std", "schi", "esilu", "cchi"])
        conv_dve = signals("conv_dve", ["u", "gch", "acc", "sq", "var", "sc", "norm", "sclo", "cc", "cclo"])
        units = range(TT * HEADS)
        att_pe = signals("att_pe", ["qT0", "qT1", "kT0", "kT1", "S0", "S1"] + [
            f"{e}{u + d}" for u in units for e, d in (("pv", -1), ("aT", 0), ("S", 2))
            if 0 <= u + d < len(units) and f"{e}{u + d}" != "pv7"] + ["pv7", "kx0", "oT0", "oT1", "kx1"])
        att_act = signals("att_act", ["elam", "q", "qT", "k", "kT", "v", "exp0"] + [
            e for u in units for e in
            ([f"exp{u + 1}"] if u + 1 < len(units) else []) + [f"aT{u}"] + (["o0"] if u == 4 else [])
            + ([f"kv{u // 2}"] if u % 2 else [])] + ["o1", "kx0", "oT0", "oT1", "kx1"])
        att_dve = signals("att_dve", ["lam2", "lam", "max0"] + [
            e for u in units for e in
            [f"a{u}"] + ([f"max{u + 1}"] if u + 1 < len(units) else []) + (["sso0", "on0"] if u == 5 else [])]
            + ["sso1", "on1", "oT0", "oT1"])
        att_pool = signals("att_pool", ["ro0", "ro1"])
        def steps(*parts):
            return [f"{name}{s + d}" for s in range(10) for name, d in parts if 0 <= s + d < 8]

        xa_pe = signals("xa_pe", ["hqT0", "S0"] + steps(("pT", 0), ("S", 1), ("pv", -1), ("oT", -2)) + ["hqT1"])
        xa_act = signals("xa_act", ["hq0", "hqT0", "exp0", "hq1"] + steps(("pT", 0), ("exp", 1), ("o", -1), ("oT", -2))
                         + ["hqT1"])
        xa_dve = signals("xa_dve", ["max0"] + steps(("rden", 0), ("max", 1), ("oT", -2)))
        for s_ in (xa_pe, xa_act):
            order = sorted(s_.order, key=s_.order.get)
            order.remove("hqT1")
            order.insert(order.index("pT1"), "hqT1")
            s_.order = {e: i for i, e in enumerate(order)}

        XA_SPLITS = {1: B_O + 1, 3: B_O + 2, 5: B_O + 3, 7: B_FFN2, 9: B_FFN2 + 1}
        XA_BLOCKS = {4: 0, 6: 1, 8: 2}

        SCALE = DK ** -0.5
        XSCALE = XD ** -0.5
        SLOPES = [2.0 ** (-8.0 * (h + 1) / HEADS) for h in range(HEADS)]
        USES = [len(range(s, NB, SLOTS)) for s in range(SLOTS)]

        def gain(norm, k):
            c = C_GAIN + 8 * NORMS.index(norm) + k
            return par[:, c:c + 1]

        def col(c):
            return par[:, c:c + 1]

        def tok(t):
            return slice(t * P, (t + 1) * P)

        def xT(k):
            bank, c = (G[2], DB[0], DB[2])[k // 2 if k < 4 else 2], (k - 4) // 2 if k > 5 else 0
            if k % 2:
                bank = (G[3], DB[1], DB[3])[k // 2 if k < 4 else 2]
            return bank[:, c * T:(c + 1) * T]

        def kv_banks(ch):
            return G[0:2] if ch % 2 == 0 else DB[2:4]

        block = ctx.enter_context(nc.Block())

        @block.sync
        def _(sp):
            def load(l, i, j=0):
                sp.dma_start(w_raw[:, i % SLOTS, :],
                             w_d[bass.ds(l * NB + j * SLOTS + i, 1)].rearrange("a p n -> (a p) n")
                             ).then_inc(w_in[i % SLOTS], 16)

            with sp.Fori(0, L) as l:
                sp.wait_ge(s_lo, FIRST + l * NB)
                sp.dma_start(par[:, :], par_d[bass.ds(l, 1)].rearrange("a p n -> (a p) n")).then_inc(s_par, 16)
                for i in range(SLOTS):
                    load(l, i)
                sp.dma_start(m_raw, memT_d).then_inc(s_mraw, 16)
                sp.dma_start(vx[:, :, :], mem_d.rearrange("(t p) n -> p t n", p=P)).then_inc(s_mem, 16)
                with sp.Fori(0, NB // SLOTS - 1) as j:
                    for i in range(SLOTS, 2 * SLOTS):
                        sp.wait_ge(s_lo, FIRST + l * NB + j * SLOTS + i - SLOTS + 1)
                        load(l, i, j)
                for i in range(NB // SLOTS * SLOTS, NB):
                    sp.wait_ge(s_lo, FIRST + l * NB + i - SLOTS + 1)
                    load(l, i)
            for t in range(TT):
                sp.wait_ge(s_fin, t + 1)
                sp.dma_start(out_d[tok(t), :], y[:, t, :]).then_inc(s_out, 16)
            sp.wait_ge(s_out, 16 * TT)

        @block.gpsimd
        def _(pool):
            def rsqrt(out, sum_sq, v, scale, n):
                nc.gpsimd.tensor_tensor(v, sum_sq, scale[:, 0:n], ALU.mult)
                pool.drain()
                nc.gpsimd.tensor_scalar(v, v, EPS, None, ALU.add)
                pool.drain()
                return nc.gpsimd.tensor_tensor(out, v, half[:, 0:n], ALU.pow)

            nc.gpsimd.memset(half[:, :], -0.5)
            nc.gpsimd.memset(over_d[:, :], 1.0 / D)
            nc.gpsimd.memset(over_dv[:, :], 1.0 / DV)
            nc.gpsimd.memset(zeros[:, :], 0.0)
            nc.gpsimd.memset(u_pad[:, :, :], 0.0)
            nc.gpsimd.memset(s_pad[:, :, :], 0.0)
            nc.gpsimd.memset(eps[:, :], EPS).then_inc(s_init, 1)
            pool.drain()

            def norm(l, phase):
                pool.wait_ge(s_ssq, l * 4 + phase + 1)
                last = rsqrt(rinv[:, :], ssq[:, :], var[:, :], over_d, TT)
                if phase == 1:
                    pool.drain()
                    last = nc.gpsimd.tensor_scalar(nrinv[:, :], rinv[:, :], -1.0, None, ALU.mult)
                last.then_inc(s_rinv, 1)

            with pool.Fori(0, L) as l:
                norm(l, 0)
                norm(l, 1)
                pool.drain()
                pool.wait_ge(s_ssm, l + 1)
                rsqrt(rmem[:, :], ssm[:, :], var[:, :], over_d, TT).then_inc(s_rmem, 1)
                pool.drain()
                for t in range(TT):
                    pool.wait_ge(att_dve.sem, att_dve.at(l, f"sso{t}"))
                    rsqrt(ro[:, t, :], sso[:, t, :], varo[:, t, :], over_dv, HEADS
                          ).then_inc(att_pool.sem, att_pool.one(f"ro{t}"))
                norm(l, 2)
                norm(l, 3)
            pool.wait_ge(s_ssq, 4 * L + 1)
            rsqrt(rinv[:, :], ssq[:, :], var[:, :], over_d, TT).then_inc(s_rinv, 1)

        @block.scalar
        def _(act):
            A = nc.scalar.activation

            def split(l, i, j=0, static=None):
                if i >= SLOTS:
                    act.wait_ge(s_blk, FIRST + l * NB + 2 * SLOTS * j + i - SLOTS + 1)
                else:
                    act.wait_ge(s_blk, FIRST + l * NB)
                s = i % SLOTS
                act.wait_ge(w_in[s], 16 * (l * USES[s] + 2 * j + i // SLOTS + 1))
                A(w_hi[:, s, :], w_raw[:, s, :], ACT.Copy).then_inc(s_hi, 1)

            def norm_start(l, phase, i):
                for k in range(KD):
                    if k == KD // 2:
                        split(l, i)
                    act.wait_ge(s_xT, l * 32 + phase * 8 + k + 1)
                    if k >= 6:
                        act.wait_ge(s_alo, l * 32 + phase * 8 + k - 1)
                    A(a_hi[:, k, :], xT(k), ACT.Copy, scale=gain(NORMS[phase], k)).then_inc(s_ahi, 1)

            def squares(l, phase):
                for t in range(TT):
                    act.drain()
                    if t == 0:
                        act.wait_ge(s_xup, FIRST + l * 16 + phase * 4)
                    last = A(junk[:, :], x[:, t, :], ACT.Square, accum_out=ssq[:, t:t + 1])
                last.then_inc(s_ssq, 1)

            def silu(l, f, j, c):
                act.wait_ge(s_blk, FIRST + l * NB + (B_FFN1, B_FFN2)[f] + 6 * j + (3 * c + 1 if c else 2))
                for t in range(TT):
                    A(sg[:, t, :], G[2 * (c % 2) + t][:, 0:CF], ACT.Silu, scale=rinv[:, t:t + 1]
                      ).then_inc(s_silu, 1)

            def hidden_hi(l, f, j, c):
                act.wait_ge(s_hT, l * 2 * STEPS + f * STEPS + 2 * j + c + 1)
                A(hT_hi[:, :, :], G[2 * (c % 2)][:, :].rearrange("p (k t) -> p k t", k=2), ACT.Copy
                  ).then_inc(s_hhi, 1)

            def ffn(l, f):
                base = (B_FFN1, B_FFN2)[f]
                norm_start(l, 3 * f, base + 2)
                squares(l, 3 * f)
                if f == 0:
                    act.wait_ge(s_mraw, 16 * l + 16)
                    for k in range(KD):
                        last = A(m_hi[:, k, :], m_raw[:, k, :], ACT.Copy, scale=gain("mem_norm", k))
                    last.then_inc(mm_.sem, mm_.one("hi"))
                act.wait_ge(s_rinv, l * 4 + 3 * f + 1)
                silu(l, f, 0, 0)
                with act.Fori(0, (STEPS - 1) // 2) as j:
                    for c in (1, 2):
                        n = base + 3 * c
                        split(l, n, j)
                        split(l, n + 1, j)
                        hidden_hi(l, f, j, c - 1)
                        split(l, n + 2, j)
                        silu(l, f, j, c)
                j = (STEPS - 1) // 2
                for i in (base + FFN_BLOCKS, base + FFN_BLOCKS + 1):
                    if i < NB:
                        split(l, i)
                hidden_hi(l, f, j, 0)

            def copy_banks(banks, out_of, n):
                for b, bank in enumerate(banks):
                    last = A(out_of(b), bank[:, 0:n], ACT.Copy)
                return last

            def mixer(l):
                norm_start(l, 1, B_IN + 2)
                squares(l, 1)
                act.wait_ge(att_dve.sem, att_dve.at(l, "lam2"))
                A(elam[:, :], lam2[:, :], ACT.Exp).then_inc(att_act.sem, att_act.one("elam"))
                act.wait_ge(s_rinv, l * 4 + 2)
                act.wait_ge(s_blk, FIRST + l * NB + B_IN + 2)
                for t in range(TT):
                    last = A(sig[:, t, :], G[t][:, CC:2 * CC], ACT.Exp, scale=nrinv[:, t:t + 1])
                last.then_inc(conv_act.sem, conv_act.one("ecg"))
                split(l, B_IN + 3)
                act.wait_ge(conv_pe.sem, conv_pe.at(l, "uT"))
                A(u_pad[:, :, KC - 1:], DB[0][:, :].rearrange("p (c t) -> p c t", c=2), ACT.Copy
                  ).then_inc(conv_act.sem, conv_act.one("uT"))
                split(l, B_IN + 4)
                act.wait_ge(s_mem, 16 * l + 16)
                for t in range(TT):
                    last = A(junk[:, :], vx[:, t, :], ACT.Square, accum_out=ssm[:, t:t + 1])
                    if t == 0:
                        act.drain()
                last.then_inc(s_ssm, 1)
                act.wait_ge(s_blk, FIRST + l * NB + B_IN + 4)
                for t in range(TT):
                    last = A(gbc[:, t, :], G[2 + t][:, :], ACT.Copy, scale=rinv[:, t:t + 1])
                last.then_inc(conv_act.sem, conv_act.one("gbc"))
                split(l, B_IN + 5)
                split(l, B_IN + 6)
                act.wait_ge(conv_pe.sem, conv_pe.at(l, "sT"))
                A(s_pad[:, :, KS - 1:], DB[1][:, :].rearrange("p (c t) -> p c t", c=2), ACT.Copy
                  ).then_inc(conv_act.sem, conv_act.one("sT"))
                act.wait_ge(conv_pe.sem, conv_pe.at(l, "gbT"))
                A(gbT[:, :, :], DB[2][:, :].rearrange("p (c t) -> p c t", c=2), ACT.Copy
                  ).then_inc(conv_act.sem, conv_act.one("gbT"))
                split(l, B_IN + 7)
                for w, name in enumerate("qk"):
                    act.wait_ge(s_blk, FIRST + l * NB + B_IN + 7 + 2 * w)
                    for t in range(TT):
                        last = A(zqk[:, w, t, :], G[2 * (1 - w) + t][:, :], ACT.Copy, scale=rinv[:, t:t + 1])
                    last.then_inc(att_act.sem, att_act.one(name))
                    split(l, B_IN + 8 + 2 * w)
                    for b in range(2):
                        act.wait_ge(att_pe.sem, att_pe.at(l, f"{name}T{b}"))
                        last = A(qkT[:, 4 * w + 2 * b:4 * w + 2 * b + 2, :],
                                 DB[(3, 0, 1, 2)[2 * w + b]][:, :].rearrange("p (h t) -> p h t", h=2), ACT.Copy)
                    last.then_inc(att_act.sem, att_act.one(f"{name}T"))
                    split(l, B_IN + 9 + 2 * w)
                act.wait_ge(s_blk, FIRST + l * NB + B_IN + 11)
                for t in range(TT):
                    last = A(v_sb[:, t, :], G[2 + t][:, :], ACT.Copy, scale=rinv[:, t:t + 1])
                last.then_inc(att_act.sem, att_act.one("v"))
                split(l, B_KV + 1)
                act.wait_ge(s_rmem, l + 1)

                def exp(u):
                    W = P * (u // HEADS + 1)
                    act.wait_ge(att_dve.sem, att_dve.at(l, f"max{u}"))
                    for c in range(2):
                        last = A(e_sb[:, u % 2, c, 0:W], s_sb[:, c, 0:W], ACT.Exp, scale=SCALE,
                                 bias=nmx[:, u % 2, c:c + 1], accum_out=den[:, u % 2, c:c + 1])
                    last.then_inc(att_act.sem, att_act.one(f"exp{u}"))

                def o_copy(t):
                    act.wait_ge(att_pe.sem, att_pe.at(l, f"pv{HEADS * t + HEADS - 1}"))
                    if t:
                        act.wait_ge(att_dve.sem, att_dve.at(l, "on0"))
                    A(o_sb[:, :, :], G[3][:, :].rearrange("p (h d) -> p h d", h=HEADS), ACT.Copy
                      ).then_inc(att_act.sem, att_act.one(f"o{t}"))

                exp(0)
                for u in units:
                    n = B_KV + u
                    if u + 1 < len(units):
                        exp(u + 1)
                    act.wait_ge(att_pe.sem, att_pe.at(l, f"aT{u}"))
                    kt = u // HEADS + 1
                    A(probT[:, 0, 0:kt, :], G[2][:, 0:kt * P].rearrange("p (k t) -> p k t", k=kt), ACT.Copy
                      ).then_inc(att_act.sem, att_act.one(f"aT{u}"))
                    if u == 4:
                        o_copy(0)
                    if u % 2:
                        act.wait_ge(s_blk, FIRST + l * NB + n + 1)
                        ch = u // 2
                        for t in range(TT):
                            last = A((kx, vx)[ch // 2][:, t, (ch % 2) * N:(ch % 2 + 1) * N], kv_banks(ch)[t][:, :],
                                     ACT.Copy, scale=rmem[:, t:t + 1])
                        last.then_inc(att_act.sem, att_act.one(f"kv{ch}"))
                    split(l, n + 2)
                    if u == 4:
                        act.wait_ge(conv_dve.sem, conv_dve.at(l, "var"))
                        A(rstd[:, :], rstd[:, :], ACT.Sqrt).then_inc(conv_act.sem, conv_act.one("std"))
                    if u == 5:
                        act.wait_ge(conv_dve.sem, conv_dve.at(l, "sc"))
                        A(a_hi[:, A_SC:A_SC + 2, :], accs[:, :, :], ACT.Copy).then_inc(conv_act.sem, conv_act.one("schi"))
                        act.wait_ge(conv_dve.sem, conv_dve.at(l, "norm"))
                        A(sq[:, :, :], acc[:, :, :], ACT.Exp, scale=-1.0
                          ).then_inc(conv_act.sem, conv_act.one("esilu"))
                    if u == 6:
                        act.wait_ge(conv_dve.sem, conv_dve.at(l, "cc"))
                        A(a_hi[:, A_CC:A_CC + 2, :], acc[:, :, :], ACT.Copy).then_inc(conv_act.sem, conv_act.one("cchi"))
                o_copy(1)

                def kx_copy(ch):
                    act.wait_ge(att_pe.sem, att_pe.at(l, f"kx{ch}"))
                    for b in range(2):
                        last = A(kxT[:, 4 * ch + 2 * b:4 * ch + 2 * b + 2, :],
                                 G[b][:, :].rearrange("p (h t) -> p h t", h=2), ACT.Copy)
                    last.then_inc(att_act.sem, att_act.one(f"kx{ch}"))

                def o_hi(t):
                    act.wait_ge(att_pe.sem, att_pe.at(l, f"oT{t}"))
                    A(a_hi[:, A_ATT:, tok(t)], G[2 + t][:, :].rearrange("p (h t) -> p h t", h=HEADS), ACT.Copy,
                      scale=gsub[:, 0:1]).then_inc(att_act.sem, att_act.one(f"oT{t}"))

                split(l, B_OUT + 2)
                kx_copy(0)
                o_hi(0)
                split(l, B_OUT + 3)
                o_hi(1)
                split(l, B_Q)
                kx_copy(1)
                split(l, B_Q + 1)

            def cross(l):
                norm_start(l, 2, B_Q + 2)
                squares(l, 2)
                act.wait_ge(s_rinv, l * 4 + 3)

                def hq_copy(ch):
                    act.wait_ge(s_blk, FIRST + l * NB + B_Q + 2 * ch + 2)
                    for t in range(TT):
                        last = A(hq[:, t, ch * N:(ch + 1) * N], G[2 * ch + t][:, :], ACT.Copy,
                                 scale=rinv[:, t:t + 1])
                    last.then_inc(xa_act.sem, xa_act.one(f"hq{ch}"))

                def hqT_copy(ch):
                    act.wait_ge(xa_pe.sem, xa_pe.at(l, f"hqT{ch}"))
                    for b in range(2):
                        last = A(hqT[:, 4 * ch + 2 * b:4 * ch + 2 * b + 2, :],
                                 DB[2 * ch + b][:, :].rearrange("p (h t) -> p h t", h=2), ACT.Copy)
                    last.then_inc(xa_act.sem, xa_act.one(f"hqT{ch}"))

                def exp(u):
                    act.wait_ge(xa_dve.sem, xa_dve.at(l, f"max{u}"))
                    A(e_x[:, u % 2, :], G[0][:, 0:T], ACT.Exp, scale=XSCALE, bias=nmx[:, u % 2, 0:1],
                      accum_out=den[:, u % 2, 0:1]).then_inc(xa_act.sem, xa_act.one(f"exp{u}"))

                def oT_hi(u):
                    h, t = u // 2, u % 2
                    act.wait_ge(xa_pe.sem, xa_pe.at(l, f"oT{u}"))
                    A(a_hi[:, 2 * h:2 * h + 2, tok(t)], G[3][:, 0:T].rearrange("p (k t) -> p k t", k=2),
                      ACT.Copy).then_inc(xa_act.sem, xa_act.one(f"oT{u}"))

                def probT_copy(u):
                    act.wait_ge(xa_pe.sem, xa_pe.at(l, f"pT{u}"))
                    A(probT[:, u % 2, :, :], G[1][:, 0:T].rearrange("p (k t) -> p k t", k=2), ACT.Copy
                      ).then_inc(xa_act.sem, xa_act.one(f"pT{u}"))

                def o_copy(u):
                    act.wait_ge(xa_dve.sem, xa_dve.at(l, f"rden{u}"))
                    act.wait_ge(xa_pe.sem, xa_pe.at(l, f"pv{u}"))
                    A(o_x[:, u % 2, :], G[2][:, 0:T], ACT.Copy, scale=rden[:, u % 2:u % 2 + 1]
                      ).then_inc(xa_act.sem, xa_act.one(f"o{u}"))

                split(l, B_Q + 3)
                hq_copy(0)
                split(l, B_O)
                hqT_copy(0)
                exp(0)
                hq_copy(1)
                for u in range(10):
                    if u == 1:
                        hqT_copy(1)
                    if u < 8:
                        probT_copy(u)
                    if u < 7:
                        exp(u + 1)
                    if 1 <= u < 9:
                        o_copy(u - 1)
                    if u >= 2:
                        oT_hi(u - 2)
                    if u in XA_SPLITS:
                        split(l, XA_SPLITS[u])

            act.dma_start(const[:, :], const_d).then_inc(s_const, 16)
            for n in range(2):
                act.dma_start(x[:, :, n * N:(n + 1) * N],
                              x_d[:, n * N:(n + 1) * N].rearrange("(t p) n -> p t n", p=P)).then_inc(s_x[n], 16)
            for n in range(2):
                act.wait_ge(s_x[n], 16)
            act.wait_ge(s_init, 1)
            with act.Fori(0, L) as l:
                act.wait_ge(s_par, 16 * l + 16)
                split(l, 0)
                split(l, 1)
                ffn(l, 0)
                mixer(l)
                cross(l)
                ffn(l, 1)
            act.dma_start(fing, fin_d).then_inc(s_fing, 16)
            squares(L, 0)

        @block.vector
        def _(dve):
            V = nc.vector

            def split(l, i, j=0):
                dve.wait_ge(s_hi, l * NB + 2 * SLOTS * j + i + 1)
                s = i % SLOTS
                V.tensor_tensor(w_lo[:, s, :], w_raw[:, s, :], w_hi[:, s, :].bitcast(F32), ALU.subtract
                                ).then_inc(s_lo, 1)

            def a_lo_part(l, phase, ks):
                for k in ks:
                    dve.wait_ge(s_ahi, l * 32 + phase * 8 + k + 1)
                    V.scalar_tensor_tensor(a_lo[:, k, :], xT(k), gain(NORMS[phase], k),
                                           a_hi[:, k, :].bitcast(F32), ALU.mult, ALU.subtract).then_inc(s_alo, 1)

            def x_update(n, factor):
                for t in range(TT):
                    xs = x[:, t, n * N:(n + 1) * N]
                    V.scalar_tensor_tensor(xs, DB[2 * n + t][:, :], factor, xs, ALU.mult, ALU.add
                                           ).then_inc(s_xup, 1)

            def first_half(l, phase, factor):
                dve.wait_ge(s_half, l * 4 + phase + 1)
                x_update(0, factor)

            def second_half(l, phase, last_block, factor, i):
                a_lo_part(l, phase + 1, range(0, 2))
                dve.wait_ge(s_blk, FIRST + l * NB + last_block + 1)
                x_update(1, factor)
                a_lo_part(l, phase + 1, range(2, 8))
                split(l, i)

            def hidden(l, f, j, c):
                dve.wait_ge(s_rinv, l * 4 + 3 * f + 1)
                for t in range(TT):
                    dve.wait_ge(s_silu, l * 4 * STEPS + f * 2 * STEPS + 4 * j + 2 * c + t + 1)
                    V.scalar_tensor_tensor(h_sb[:, t, :], G[2 * (c % 2) + t][:, CF:2 * CF], rinv[:, t:t + 1],
                                           sg[:, t, :], ALU.mult, ALU.mult).then_inc(s_h, 1)

            def hidden_lo(l, f, j, c):
                dve.wait_ge(s_hhi, l * 2 * STEPS + f * STEPS + 2 * j + c + 1)
                V.tensor_tensor(hT_lo[:, :, :], G[2 * (c % 2)][:, :].rearrange("p (k t) -> p k t", k=2),
                                hT_hi[:, :, :].bitcast(F32), ALU.subtract).then_inc(s_hlo, 1)

            def ffn(l, f):
                base = (B_FFN1, B_FFN2)[f]
                if f == 0:
                    a_lo_part(l, 0, range(8))
                    split(l, 2)
                    dve.wait_ge(mm_.sem, mm_.at(l, "hi"))
                    for k in range(KD):
                        last = V.scalar_tensor_tensor(m_lo[:, k, :], m_raw[:, k, :], gain("mem_norm", k),
                                                      m_hi[:, k, :].bitcast(F32), ALU.mult, ALU.subtract)
                    last.then_inc(mm_.sem, mm_.one("lo"))
                hidden(l, f, 0, 0)
                with dve.Fori(0, (STEPS - 1) // 2) as j:
                    for c in (1, 2):
                        n = base + 3 * c
                        split(l, n, j)
                        split(l, n + 1, j)
                        hidden_lo(l, f, j, c - 1)
                        split(l, n + 2, j)
                        hidden(l, f, j, c)
                j = (STEPS - 1) // 2
                for i in (base + FFN_BLOCKS, base + FFN_BLOCKS + 1):
                    if i < NB:
                        split(l, i)
                hidden_lo(l, f, j, 0)
                first_half(l, 3 * f, 0.5)
                if f == 0:
                    second_half(l, 0, B_IN - 1, 0.5, B_IN + 2)
                else:
                    dve.wait_ge(s_blk, FIRST + l * NB + NB)
                    x_update(1, 0.5)

            def mixer(l):
                for i in range(2):
                    q, k = C_LAM + 2 * i * DK, C_LAM + (2 * i + 1) * DK
                    last = V.scalar_tensor_tensor(lamj[:, i, :], par[:, q:q + DK], 1.0, par[:, k:k + DK],
                                                  ALU.mult, ALU.mult, accum_out=lam2[:, i:i + 1])
                last.then_inc(att_dve.sem, att_dve.one("lam2"))
                V.tensor_scalar(gsub[:, :], col(C_SUB), col(C_REST), None, ALU.mult)
                dve.wait_ge(att_act.sem, att_act.at(l, "elam"))
                V.scalar_tensor_tensor(lam[:, :], elam[:, 0:1], col(C_INIT), elam[:, 1:2], ALU.add, ALU.subtract
                                       ).then_inc(att_dve.sem, att_dve.one("lam"))
                dve.wait_ge(s_rinv, l * 4 + 2)
                dve.wait_ge(conv_act.sem, conv_act.at(l, "ecg"))
                V.tensor_scalar(sig[:, :, :], sig[:, :, :], 1.0, None, ALU.add)
                dve.drain()
                V.reciprocal(sig[:, :, :], sig[:, :, :])
                dve.drain()
                for t in range(TT):
                    last = V.scalar_tensor_tensor(u_sb[:, t, :], G[t][:, 0:CC], rinv[:, t:t + 1], sig[:, t, :],
                                                  ALU.mult, ALU.mult)
                last.then_inc(conv_dve.sem, conv_dve.one("u"))
                split(l, B_IN + 3)

                def taps(ks):
                    for j in ks:
                        for c in range(2):
                            w = col(C_CCW + c * KC + j)
                            src = u_pad[:, c, j:j + T]
                            if j == 0:
                                V.tensor_scalar(acc[:, c, :], src, w, col(C_CCB + c), ALU.mult, ALU.add)
                            else:
                                last = V.scalar_tensor_tensor(acc[:, c, :], src, w, acc[:, c, :], ALU.mult, ALU.add)
                        if j == KC - 1:
                            last.then_inc(conv_dve.sem, conv_dve.one("acc"))
                        dve.drain()

                split(l, B_IN + 4)
                dve.wait_ge(conv_act.sem, conv_act.at(l, "uT"))
                taps(range(0, 3))
                split(l, B_IN + 5)
                taps(range(3, 6))
                dve.wait_ge(conv_act.sem, conv_act.at(l, "gbc"))
                dve.wait_ge(s_blk, FIRST + l * NB + B_IN + 5)
                for t in range(TT):
                    last = V.scalar_tensor_tensor(gch[:, t, :], G[t][:, 0:CC], rinv[:, t:t + 1],
                                                  gbc[:, t, CC:2 * CC], ALU.mult, ALU.mult)
                last.then_inc(conv_dve.sem, conv_dve.one("gch"))
                split(l, B_IN + 6)
                taps(range(6, 9))
                for n in range(5):
                    split(l, B_IN + 7 + n)
                    taps(range(9 + 4 * n, 13 + 4 * n))

                def scores(u):
                    t, h = u // HEADS, u % HEADS
                    W = P * (t + 1)
                    dve.wait_ge(att_pe.sem, att_pe.at(l, f"S{u}"))
                    if u:
                        dve.wait_ge(att_act.sem, att_act.at(l, f"exp{u - 1}"))
                    dist = const[:, K_DIST + t * T:K_DIST + t * T + W]
                    for c in range(2):
                        V.scalar_tensor_tensor(s_sb[:, c, 0:W], dist, -SLOPES[h] / SCALE, DB[c][:, 0:W],
                                               ALU.mult, ALU.add)
                    dve.drain()
                    V.reduce_max(mx[:, :], s_sb[:, :, 0:W], AX_X)
                    dve.drain()
                    V.tensor_scalar(nmx[:, u % 2, :], mx[:, :], -SCALE, None, ALU.mult
                                    ).then_inc(att_dve.sem, att_dve.one(f"max{u}"))

                def combine(u):
                    W = P * (u // HEADS + 1)
                    dve.wait_ge(att_act.sem, att_act.at(l, f"exp{u}"))
                    V.reciprocal(rden[:, :], den[:, u % 2, :])
                    dve.drain()
                    V.tensor_scalar(rden[:, 1:2], rden[:, 1:2], lam[:, 0:1], None, ALU.mult)
                    dve.drain()
                    V.tensor_scalar(e_sb[:, u % 2, 1, 0:W], e_sb[:, u % 2, 1, 0:W], rden[:, 1:2], None, ALU.mult)
                    dve.drain()
                    if u:
                        dve.wait_ge(att_pe.sem, att_pe.at(l, f"aT{u - 1}"))
                    V.scalar_tensor_tensor(prob[:, 0:W], e_sb[:, u % 2, 0, 0:W], rden[:, 0:1],
                                           e_sb[:, u % 2, 1, 0:W], ALU.mult, ALU.subtract
                                           ).then_inc(att_dve.sem, att_dve.one(f"a{u}"))

                def o_norm(t):
                    dve.wait_ge(att_act.sem, att_act.at(l, f"o{t}"))
                    for h in range(HEADS):
                        last = V.scalar_tensor_tensor(on_sb[:, t, h, :], o_sb[:, h, :], 1.0, o_sb[:, h, :],
                                                      ALU.mult, ALU.mult, accum_out=sso[:, t, h:h + 1])
                    last.then_inc(att_dve.sem, att_dve.one(f"sso{t}"))
                    dve.wait_ge(att_pool.sem, att_pool.at(l, f"ro{t}"))
                    for h in range(HEADS):
                        last = V.tensor_scalar(on_sb[:, t, h, :], o_sb[:, h, :], ro[:, t, h:h + 1], None, ALU.mult)
                    last.then_inc(att_dve.sem, att_dve.one(f"on{t}"))

                scores(0)
                split(l, B_KV + 1)
                for u in units:
                    combine(u)
                    if u + 1 < len(units):
                        scores(u + 1)
                    if u == 1:
                        taps(range(29, 31))
                    if u == 3:
                        dve.wait_ge(conv_pe.sem, conv_pe.at(l, "mean"))
                        for c in range(2):
                            V.tensor_tensor(acc[:, c, :], acc[:, c, :], G[0][:, 0:T], ALU.subtract)
                        dve.drain()
                        V.tensor_tensor(sq[:, :, :], acc[:, :, :], acc[:, :, :], ALU.mult
                                        ).then_inc(conv_dve.sem, conv_dve.one("sq"))
                        split(l, B_KV + u + 2)
                        dve.wait_ge(conv_pe.sem, conv_pe.at(l, "var"))
                        V.tensor_scalar(rstd[:, :], G[1][:, 0:T], EPS, None, ALU.add
                                        ).then_inc(conv_dve.sem, conv_dve.one("var"))
                    if u == 4:
                        dve.wait_ge(conv_act.sem, conv_act.at(l, "gbT"))
                        for j in range(KS):
                            for c in range(2):
                                w = col(C_SCW + c * KS + j)
                                src = s_pad[:, c, j:j + T]
                                if j == 0:
                                    V.tensor_scalar(accs[:, c, :], src, w, None, ALU.mult)
                                else:
                                    V.scalar_tensor_tensor(accs[:, c, :], src, w, accs[:, c, :], ALU.mult, ALU.add)
                            dve.drain()
                        V.tensor_tensor(accs[:, :, :], accs[:, :, :], gbT[:, :, :], ALU.mult
                                        ).then_inc(conv_dve.sem, conv_dve.one("sc"))
                    if u == 5:
                        dve.wait_ge(conv_act.sem, conv_act.at(l, "std"))
                        V.reciprocal(rstd[:, :], rstd[:, :])
                        dve.drain()
                        for c in range(2):
                            V.tensor_tensor(acc[:, c, :], acc[:, c, :], rstd[:, :], ALU.mult)
                        dve.drain()
                        for c in range(2):
                            last = V.tensor_scalar(acc[:, c, :], acc[:, c, :], col(C_LNG + c), col(C_LNB + c),
                                                   ALU.mult, ALU.add)
                        last.then_inc(conv_dve.sem, conv_dve.one("norm"))
                        o_norm(0)
                    if u == 6:
                        dve.wait_ge(conv_act.sem, conv_act.at(l, "schi"))
                        V.tensor_tensor(a_lo[:, A_SC:A_SC + 2, :], accs[:, :, :],
                                        a_hi[:, A_SC:A_SC + 2, :].bitcast(F32), ALU.subtract
                                        ).then_inc(conv_dve.sem, conv_dve.one("sclo"))
                        dve.wait_ge(conv_act.sem, conv_act.at(l, "esilu"))
                        V.tensor_scalar(sq[:, :, :], sq[:, :, :], 1.0, None, ALU.add)
                        dve.drain()
                        V.reciprocal(sq[:, :, :], sq[:, :, :])
                        dve.drain()
                        V.tensor_tensor(acc[:, :, :], acc[:, :, :], sq[:, :, :], ALU.mult
                                        ).then_inc(conv_dve.sem, conv_dve.one("cc"))
                    if u != 3:
                        split(l, B_KV + u + 2)
                dve.wait_ge(conv_act.sem, conv_act.at(l, "cchi"))
                V.tensor_tensor(a_lo[:, A_CC:A_CC + 2, :], acc[:, :, :],
                                a_hi[:, A_CC:A_CC + 2, :].bitcast(F32), ALU.subtract
                                ).then_inc(conv_dve.sem, conv_dve.one("cclo"))

                def o_lo(t):
                    dve.wait_ge(att_act.sem, att_act.at(l, f"oT{t}"))
                    V.scalar_tensor_tensor(a_lo[:, A_ATT:, tok(t)], G[2 + t][:, :].rearrange("p (h t) -> p h t", h=HEADS),
                                           gsub[:, 0:1], a_hi[:, A_ATT:, tok(t)].bitcast(F32), ALU.mult, ALU.subtract
                                           ).then_inc(att_dve.sem, att_dve.one(f"oT{t}"))

                o_norm(1)
                split(l, B_OUT + 2)
                o_lo(0)
                split(l, B_OUT + 3)
                o_lo(1)
                split(l, B_Q)
                split(l, B_Q + 1)
                first_half(l, 1, 1.0)
                second_half(l, 1, B_OUT + 3, 1.0, B_Q + 2)

            def cross(l):
                split(l, B_Q + 3)
                split(l, B_O)

                def row_max(u):
                    dve.wait_ge(xa_pe.sem, xa_pe.at(l, f"S{u}"))
                    V.reduce_max(mx[:, u % 2:u % 2 + 1], G[0][:, 0:T], AX_X)
                    dve.drain()
                    V.tensor_scalar(nmx[:, u % 2, 0:1], mx[:, u % 2:u % 2 + 1], -XSCALE, None, ALU.mult
                                    ).then_inc(xa_dve.sem, xa_dve.one(f"max{u}"))

                def oT_lo(u):
                    h, t = u // 2, u % 2
                    dve.wait_ge(xa_act.sem, xa_act.at(l, f"oT{u}"))
                    V.tensor_tensor(a_lo[:, 2 * h:2 * h + 2, tok(t)],
                                    G[3][:, 0:T].rearrange("p (k t) -> p k t", k=2),
                                    a_hi[:, 2 * h:2 * h + 2, tok(t)].bitcast(F32), ALU.subtract
                                    ).then_inc(xa_dve.sem, xa_dve.one(f"oT{u}"))

                row_max(0)
                for u in range(10):
                    if u < 8:
                        dve.wait_ge(xa_act.sem, xa_act.at(l, f"exp{u}"))
                        V.reciprocal(rden[:, u % 2:u % 2 + 1], den[:, u % 2, 0:1]
                                     ).then_inc(xa_dve.sem, xa_dve.one(f"rden{u}"))
                    if u < 7:
                        row_max(u + 1)
                    if u >= 2:
                        oT_lo(u - 2)
                    if u in XA_SPLITS:
                        split(l, XA_SPLITS[u])
                first_half(l, 2, 1.0)
                second_half(l, 2, B_O + 3, 1.0, B_FFN2 + 2)

            lamj = v_sb[:, 0, 0:2 * DK].rearrange("p (a k) -> p a k", a=2)
            dve.sem_inc(s_lo, FIRST)
            dve.sem_inc(s_xup, FIRST)
            dve.wait_ge(s_init, 1)
            dve.wait_ge(s_const, 16)
            for n in range(2):
                dve.wait_ge(s_x[n], 16)
            with dve.Fori(0, L) as l:
                dve.wait_ge(s_par, 16 * l + 16)
                split(l, 0)
                split(l, 1)
                ffn(l, 0)
                mixer(l)
                cross(l)
                ffn(l, 1)
            dve.wait_ge(s_fing, 16)
            dve.wait_ge(s_rinv, 4 * L + 1)
            for t in range(TT):
                V.scalar_tensor_tensor(y[:, t, :], x[:, t, :], rinv[:, t:t + 1], fing, ALU.mult, ALU.mult
                                       ).then_inc(s_fin, 1)

        @block.tensor
        def _(pe):
            M = nc.tensor.matmul
            TR = nc.tensor.transpose

            def weights(l, i, j=0):
                pe.wait_ge(s_lo, FIRST + l * NB + 2 * SLOTS * j + i + 1)
                return w_hi[:, i % SLOTS, :], w_lo[:, i % SLOTS, :]

            def product(out, hi, lo, whi, wlo, start, stop):
                M(out, hi, whi, start=start, stop=False)
                M(out, hi, wlo, start=False, stop=False)
                return M(out, lo, whi, start=False, stop=stop)

            def wide(l, i, ahi, alo, banks, ks, width=N, j=0, ready=None, between=None):
                whi, wlo = weights(l, i, j)
                for n, k in enumerate(ks):
                    if n == 2 and between is not None:
                        between()
                    if ready is not None:
                        pe.wait_ge(s_alo, ready + k + 1)
                    for t in range(TT):
                        last = product(banks[t][:, 0:width], ahi[:, k, tok(t)], alo[:, k, tok(t)],
                                       whi[:, n * width:(n + 1) * width], wlo[:, n * width:(n + 1) * width],
                                       k == 0, k == KD - 1)
                last.then_inc(s_blk, 1)

            def down(l, i, hi, lo, ks, start, stop, j=0, between=None):
                whi, wlo = weights(l, i, j)
                for n, k in enumerate(ks):
                    if n == 1 and between is not None:
                        between()
                    for c in range(2):
                        w = slice(n * D + c * N, n * D + (c + 1) * N)
                        for t in range(TT):
                            last = product(DB[2 * c + t][:, :], hi[:, k, tok(t)], lo[:, k, tok(t)], whi[:, w],
                                           wlo[:, w], start and n == 0, stop and n == 1)
                last.then_inc(s_blk, 1)

            def last_down(l, i, hi, lo, ks, phase):
                whi, wlo = weights(l, i)
                for c in range(2):
                    for n, k in enumerate(ks):
                        w = slice(n * D + c * N, n * D + (c + 1) * N)
                        for t in range(TT):
                            if (c, n, t) == (1, 1, 1):
                                pe.wait_ge(s_xup, FIRST + l * 16 + phase * 4 + 2)
                                x_transposes(range(4))
                            last = product(DB[2 * c + t][:, :], hi[:, k, tok(t)], lo[:, k, tok(t)], whi[:, w],
                                           wlo[:, w], False, n == 1)
                    if c == 0:
                        last.then_inc(s_half, 1)
                last.then_inc(s_blk, 1)

            def x_transposes(ks):
                for k in ks:
                    for t in range(TT):
                        last = TR(xT(k)[:, tok(t)], x[:, t, k * P:(k + 1) * P], ident)
                    if k < 4:
                        last.then_inc(s_xT, 1)
                if ks[-1] == 7:
                    last.then_inc(s_xT, 4)

            def first_blocks(l, i, phase):
                def second_half():
                    pe.wait_ge(s_xup, FIRST + l * 16 + phase * 4)
                    x_transposes(range(4, 8))

                ready = l * 32 + phase * 8
                wide(l, i, a_hi, a_lo, G[0:2], range(4), ready=ready, between=second_half)
                wide(l, i + 1, a_hi, a_lo, G[0:2], range(4, 8), ready=ready)

            def transpose_pairs(src, banks, signals_, names):
                for b, bank in enumerate(banks):
                    for i in range(2):
                        for t in range(TT):
                            last = TR(bank[:, i * T + t * P:i * T + (t + 1) * P], src(t, 2 * b + i), ident)
                    if names[b]:
                        last.then_inc(signals_.sem, signals_.one(names[b]))

            def ffn(l, f):
                base = (B_FFN1, B_FFN2)[f]
                first_blocks(l, base, 3 * f)
                for b in range(4):
                    M(DB[b][:, :], zeros[:, 0:P], zeros[:, :], start=True, stop=False)

                def transposes(j, c):
                    pe.wait_ge(s_h, l * 4 * STEPS + f * 2 * STEPS + 4 * j + 2 * c + 2)
                    for k in range(2):
                        for t in range(TT):
                            last = TR(G[2 * (c % 2)][:, k * T + t * P:k * T + (t + 1) * P],
                                      h_sb[:, t, k * P:(k + 1) * P], ident)
                    last.then_inc(s_hT, 1)

                def hidden_ready(j, c):
                    pe.wait_ge(s_hlo, l * 2 * STEPS + f * STEPS + 2 * j + c + 1)

                with pe.Fori(0, (STEPS - 1) // 2) as j:
                    for c in (1, 2):
                        n = base + 3 * c
                        banks = G[2 * (c % 2):2 * (c % 2) + 2]
                        wide(l, n - 1, a_hi, a_lo, banks, range(4), j=j)
                        transposes(j, c - 1)
                        wide(l, n, a_hi, a_lo, banks, range(4, 8), j=j)
                        hidden_ready(j, c - 1)
                        down(l, n + 1, hT_hi, hT_lo, range(2), False, False, j=j)
                j = (STEPS - 1) // 2
                transposes(j, 0)
                hidden_ready(j, 0)
                last_down(l, base + FFN_BLOCKS - 1, hT_hi, hT_lo, range(2), 3 * f)

            def mixer(l):
                first_blocks(l, B_IN, 1)
                wide(l, B_IN + 2, a_hi, a_lo, G[2:4], range(4))
                pe.wait_ge(conv_dve.sem, conv_dve.at(l, "u"))
                transpose_pairs(lambda t, i: u_sb[:, t, i * P:(i + 1) * P], [DB[0]], conv_pe, ["uT"])
                wide(l, B_IN + 3, a_hi, a_lo, G[2:4], range(4, 8))
                wide(l, B_IN + 4, a_hi, a_lo, G[0:2], range(8), width=CC)
                pe.wait_ge(conv_act.sem, conv_act.at(l, "gbc"))
                wide(l, B_IN + 5, a_hi, a_lo, G[2:4], range(4))
                pe.wait_ge(conv_dve.sem, conv_dve.at(l, "gch"))
                transpose_pairs(lambda t, i: gch[:, t, i * P:(i + 1) * P], [DB[1]], conv_pe, ["sT"])
                transpose_pairs(lambda t, i: gbc[:, t, i * P:(i + 1) * P], [DB[2]], conv_pe, ["gbT"])
                wide(l, B_IN + 6, a_hi, a_lo, G[2:4], range(4, 8))
                wide(l, B_IN + 7, a_hi, a_lo, G[0:2], range(4))
                pe.wait_ge(att_act.sem, att_act.at(l, "q"))
                transpose_pairs(lambda t, i: zqk[:, 0, t, i * P:(i + 1) * P], [DB[3], DB[0]], att_pe, ["qT0", "qT1"])
                wide(l, B_IN + 8, a_hi, a_lo, G[0:2], range(4, 8))
                wide(l, B_IN + 9, a_hi, a_lo, G[2:4], range(4))
                pe.wait_ge(conv_act.sem, conv_act.at(l, "gbT"))
                pe.wait_ge(att_act.sem, att_act.at(l, "k"))
                transpose_pairs(lambda t, i: zqk[:, 1, t, i * P:(i + 1) * P], [DB[1], DB[2]], att_pe, ["kT0", "kT1"])
                wide(l, B_IN + 10, a_hi, a_lo, G[2:4], range(4, 8))

                def S(u):
                    t, h = u // HEADS, u % HEADS
                    W = P * (t + 1)
                    if u:
                        pe.wait_ge(att_dve.sem, att_dve.at(l, f"max{u - 1}"))
                    for c in range(2):
                        r = slice(c * DK, (c + 1) * DK)
                        last = M(DB[c][:, 0:W], qkT[r, h, tok(t)], qkT[r, HEADS + h, 0:W], start=True, stop=True)
                    last.then_inc(att_pe.sem, att_pe.one(f"S{u}"))

                def aT(u):
                    pe.wait_ge(att_dve.sem, att_dve.at(l, f"a{u}"))
                    for k in range(u // HEADS + 1):
                        last = TR(G[2][:, k * P:(k + 1) * P], prob[:, k * P:(k + 1) * P], ident)
                    last.then_inc(att_pe.sem, att_pe.one(f"aT{u}"))

                def pv(u):
                    t, h = u // HEADS, u % HEADS
                    pe.wait_ge(att_act.sem, att_act.at(l, f"aT{u}"))
                    if u == HEADS:
                        pe.wait_ge(att_act.sem, att_act.at(l, "o0"))
                    for k in range(t + 1):
                        last = M(G[3][:, h * DV:(h + 1) * DV], probT[:, 0, k, :], v_sb[:, k, h * DV:(h + 1) * DV],
                                 start=(k == 0), stop=(k == t))
                    last.then_inc(att_pe.sem, att_pe.one(f"pv{u}"))

                pe.wait_ge(att_act.sem, att_act.at(l, "kT"))
                S(0)
                pe.wait_ge(mm_.sem, mm_.at(l, "lo"))
                for u in units:
                    n = B_KV + u
                    if u in (4, 6):
                        pe.wait_ge(att_act.sem, att_act.at(l, f"kv{u // 2 - 2}"))
                    if u == 4:
                        pe.wait_ge(conv_dve.sem, conv_dve.at(l, "var"))
                    if u == 0:
                        S(1)
                    wide(l, n, m_hi, m_lo, kv_banks(u // 2), range(4 * (u % 2), 4 * (u % 2) + 4))
                    if u == 3:
                        pe.wait_ge(conv_dve.sem, conv_dve.at(l, "sq"))
                        for c in range(2):
                            last = M(G[1][:, 0:T], mean_w, sq[:, c, :], start=(c == 0), stop=(c == 1))
                        last.then_inc(conv_pe.sem, conv_pe.one("var"))
                    if u:
                        pv(u - 1)
                    if u == 0:
                        pe.wait_ge(att_act.sem, att_act.at(l, "v"))
                    aT(u)
                    if u + 2 < len(units):
                        S(u + 2)
                    if u == 2:
                        pe.wait_ge(att_act.sem, att_act.at(l, "kv0"))
                        pe.wait_ge(conv_dve.sem, conv_dve.at(l, "acc"))
                        for c in range(2):
                            last = M(G[0][:, 0:T], mean_w, acc[:, c, :], start=(c == 0), stop=(c == 1))
                        last.then_inc(conv_pe.sem, conv_pe.one("mean"))

                def out(i, between=None):
                    k = 2 * A_PAIR[i]
                    down(l, B_OUT + i, a_hi, a_lo, (k, k + 1), i == 0, False, between=between)

                def kx_transposes(ch):
                    transpose_pairs(lambda t, i: kx[:, t, (4 * ch + i) * P:(4 * ch + i + 1) * P], [G[0], G[1]],
                                    att_pe, [None, f"kx{ch}"])

                def o_transposes(t):
                    pe.wait_ge(att_dve.sem, att_dve.at(l, f"on{t}"))
                    for h in range(HEADS):
                        last = TR(G[2 + t][:, h * P:(h + 1) * P], on_sb[:, t, h, :], ident)
                    last.then_inc(att_pe.sem, att_pe.one(f"oT{t}"))

                pe.wait_ge(conv_dve.sem, conv_dve.at(l, "sclo"))
                pe.wait_ge(att_act.sem, att_act.at(l, "kv3"))
                out(0, between=lambda: pv(7))
                kx_transposes(0)
                o_transposes(0)
                pe.wait_ge(conv_dve.sem, conv_dve.at(l, "cclo"))
                out(1)
                o_transposes(1)
                pe.wait_ge(att_act.sem, att_act.at(l, "kx0"))
                kx_transposes(1)
                pe.wait_ge(att_dve.sem, att_dve.at(l, "oT1"))
                out(2)
                k = 2 * A_PAIR[3]
                last_down(l, B_OUT + 3, a_hi, a_lo, (k, k + 1), 1)

            def cross(l):
                pe.wait_ge(att_act.sem, att_act.at(l, "kx1"))
                first_blocks(l, B_Q, 2)
                wide(l, B_Q + 2, a_hi, a_lo, G[2:4], range(4))

                def hq_transposes(ch):
                    pe.wait_ge(xa_act.sem, xa_act.at(l, f"hq{ch}"))
                    transpose_pairs(lambda t, i: hq[:, t, (4 * ch + i) * P:(4 * ch + i + 1) * P],
                                    [DB[2 * ch], DB[2 * ch + 1]], xa_pe, [None, f"hqT{ch}"])

                def S(u):
                    h, t = u // 2, u % 2
                    if u == 0:
                        pe.wait_ge(xa_act.sem, xa_act.at(l, "hqT0"))
                    if u == 4:
                        pe.wait_ge(xa_act.sem, xa_act.at(l, "hqT1"))
                    for k in range(2):
                        last = M(G[0][:, 0:T], hqT[:, 2 * h + k, tok(t)], kxT[:, 2 * h + k, :],
                                 start=(k == 0), stop=(k == 1))
                    last.then_inc(xa_pe.sem, xa_pe.one(f"S{u}"))

                def pT(u):
                    pe.wait_ge(xa_act.sem, xa_act.at(l, f"exp{u}"))
                    for k in range(2):
                        last = TR(G[1][:, k * P:(k + 1) * P], e_x[:, u % 2, k * P:(k + 1) * P], ident)
                    last.then_inc(xa_pe.sem, xa_pe.one(f"pT{u}"))

                def pv(u):
                    pe.wait_ge(xa_act.sem, xa_act.at(l, f"pT{u}"))
                    if u:
                        pe.wait_ge(xa_act.sem, xa_act.at(l, f"o{u - 1}"))
                    for k in range(2):
                        last = M(G[2][:, 0:XD], probT[:, u % 2, k, :], vx[:, k, (u // 2) * XD:(u // 2 + 1) * XD],
                                 start=(k == 0), stop=(k == 1))
                    last.then_inc(xa_pe.sem, xa_pe.one(f"pv{u}"))

                def oT(u):
                    pe.wait_ge(xa_act.sem, xa_act.at(l, f"o{u}"))
                    if u:
                        pe.wait_ge(xa_dve.sem, xa_dve.at(l, f"oT{u - 1}"))
                    for k in range(2):
                        last = TR(G[3][:, k * P:(k + 1) * P], o_x[:, u % 2, k * P:(k + 1) * P], ident)
                    last.then_inc(xa_pe.sem, xa_pe.one(f"oT{u}"))

                hq_transposes(0)
                wide(l, B_Q + 3, a_hi, a_lo, G[2:4], range(4, 8), between=lambda: S(0))
                for u in range(10):
                    if u == 1:
                        hq_transposes(1)
                    if u < 8:
                        pT(u)
                    if u < 7:
                        S(u + 1)
                    if 1 <= u < 9:
                        pv(u - 1)
                    if 2 <= u < 9:
                        oT(u - 2)
                    if u in XA_BLOCKS:
                        b = XA_BLOCKS[u]
                        pe.wait_ge(xa_dve.sem, xa_dve.at(l, f"oT{2 * b + 1}"))
                        down(l, B_O + b, a_hi, a_lo, (2 * b, 2 * b + 1), b == 0, False,
                             between=(lambda: oT(7)) if b == 2 else None)
                pe.wait_ge(xa_dve.sem, xa_dve.at(l, "oT7"))
                last_down(l, B_O + 3, a_hi, a_lo, (6, 7), 2)

            pe.sem_inc(s_blk, FIRST)
            pe.wait_ge(s_const, 16)
            pe.wait_ge(s_init, 1)
            pe.wait_ge(s_x[0], 16)
            x_transposes(range(4))
            pe.wait_ge(s_x[1], 16)
            with pe.Fori(0, L) as l:
                ffn(l, 0)
                mixer(l)
                cross(l)
                ffn(l, 1)


def kernel(**inputs):
    import numpy as np
    import concourse.bacc as bacc
    from concourse.bass_utils import run_bass_kernel_spmd

    a = {k: np.asarray(v) for k, v in inputs.items()}

    def chunks(w, cols):
        k = w.shape[0] // P
        return w.reshape(k, P, cols).transpose(1, 0, 2).reshape(P, k * cols)

    stream = np.empty((L * NB, P, BLOCK), np.float32)
    at = 0

    def put(w):
        nonlocal at
        stream[at] = chunks(w, w.shape[1])
        at += 1

    def put_wide(w):
        put(w[:D // 2])
        put(w[D // 2:])

    for l in range(L):
        def ffn(n):
            gate, up, down = (a[f"ffn{n}_w_{k}"][l] for k in ("gate", "up", "down"))
            for c in range(STEPS + 1):
                s = slice(c * CF, (c + 1) * CF)
                if c < STEPS:
                    put_wide(np.concatenate([gate[:, s], up[:, s]], 1))
                if c:
                    put(down[(c - 1) * CF:c * CF])

        ffn(1)
        w = a["w_in"][l]
        for c in (3 * N, 4 * N):
            put_wide(w[:, c:c + N])
        put(w[:, 5 * N:5 * N + CC])
        for c in (0, N, 2 * N):
            put_wide(w[:, c:c + N])
        for c in range(0, 2 * D, N):
            put_wide(a["xa_wkv"][l][:, c:c + N])
        for k in OUT_ORDER:
            put(a["w_out"][l][k * 2 * P:(k + 1) * 2 * P])
        for c in (0, N):
            put_wide(a["xa_wq"][l][:, c:c + N])
        for k in range(4):
            put(a["xa_wo"][l][k * 2 * P:(k + 1) * 2 * P])
        ffn(2)
    assert at == L * NB

    par = np.empty((L, P, NPAR), np.float32)
    for l in range(L):
        for n, name in enumerate(NORMS):
            par[l, :, C_GAIN + 8 * n:C_GAIN + 8 * n + 8] = a[name][l].reshape(8, P).T
        par[l, :, C_SUB] = a["diff_subln"][l]
        for c in range(2):
            ch = slice(c * P, (c + 1) * P)
            par[l, :, C_CCW + c * KC:C_CCW + (c + 1) * KC] = a["cc_dw"][l][:, ch].T
            par[l, :, C_CCB + c] = a["cc_dw_b"][l][ch]
            par[l, :, C_LNG + c] = a["cc_ln_g"][l][ch]
            par[l, :, C_LNB + c] = a["cc_ln_b"][l][ch]
            par[l, :, C_SCW + c * KS:C_SCW + (c + 1) * KS] = a["sc_dw"][l][:, ch].T
        for n, name in enumerate(("lam_q1", "lam_k1", "lam_q2", "lam_k2")):
            par[l, :, C_LAM + n * DK:C_LAM + (n + 1) * DK] = a[name][l]
        par[l, :, C_INIT] = 0.8 - 0.6 * float(np.exp(-0.3 * l))
        par[l, :, C_REST] = 1.0 - (0.8 - 0.6 * float(np.exp(-0.3 * l)))

    const = np.zeros((P, NCONST), np.float32)
    const[:, K_ID:K_ID + P] = np.eye(P)
    const[:, K_MEAN:K_MEAN + P] = 1.0 / CC
    for t in range(TT):
        dist = (t * P + np.arange(P))[:, None] - np.arange(T)[None, :]
        const[:, K_DIST + t * T:K_DIST + (t + 1) * T] = np.where(dist >= 0, dist, MASKED)

    arrays = {
        "x_dram": np.ascontiguousarray(a["x"].reshape(T, D)),
        "mem_dram": np.ascontiguousarray(a["mem"].reshape(T, D)),
        "memT_dram": np.ascontiguousarray(a["mem"].reshape(T, KD, P).transpose(2, 1, 0)),
        "w_dram": stream,
        "par_dram": par,
        "const_dram": const,
        "fin_dram": np.ascontiguousarray(np.broadcast_to(a["final_norm"][None, :], (P, D))),
    }
    nc = bacc.Bacc("TRN2", target_bir_lowering=False, num_devices=1)
    args = [nc.dram_tensor(k, v.shape, F32, kind="ExternalInput").ap() for k, v in arrays.items()]
    out = nc.dram_tensor("out_dram", (T, D), F32, kind="ExternalOutput").ap()
    hymba_kernel(nc, *args, out)
    r = run_bass_kernel_spmd(nc, [arrays], core_ids=[0])
    return r.results[0]["out_dram"].reshape(1, T, D)
```

```python
from contextlib import ExitStack

import concourse.bass as bass
from concourse import mybir

F32 = mybir.dt.float32
F32R = mybir.dt.float32r
BF16 = mybir.dt.bfloat16
ALU = mybir.AluOpType
ACT = mybir.ActivationFunctionType
AX_X = mybir.AxisListType.X

P = 128
EPS = 1e-6
NORMS = ("ffn1_norm", "mix_norm", "xa_norm", "ffn2_norm", "mem_norm")

D, T, L, F = 1024, 256, 2, 2816
HEADS, DK, DV = 4, 64, 128
CC, KC, KS = 256, 31, 3
XH, XD = 4, 256
KD = D // P
TT = T // P
N = 512
CF = N // 2
STEPS = F // CF
PAIRS = (STEPS - 3) // 2
BLOCK = 2048
SLOTS = 3
FIRST = 4

AHEAD = 2
FFN_BLOCKS = 3 * STEPS
PIECES = ((0, 1), (1, 2), (2, 4))
B_FFN1 = len(PIECES) - 1
B_IN = B_FFN1 + FFN_BLOCKS
B_KV = B_IN + 11
B_OUT = B_KV + 8
B_Q = B_OUT + 4
B_O = B_Q + 4
B_FFN2 = B_O + 4
NB = B_FFN2 + FFN_BLOCKS
assert NB % SLOTS == 0
ROUNDS = NB // SLOTS
OUT_ORDER = (3, 2, 0, 1)
A_PAIR = (1, 0, 2, 3)
A_CC, A_SC, A_ATT = 0, 2, 4

C_GAIN = 0
C_SUB = C_GAIN + 8 * len(NORMS)
C_CCW = C_SUB + 1
C_CCB = C_CCW + 2 * KC
C_LNG = C_CCB + 2
C_LNB = C_LNG + 2
C_SCW = C_LNB + 2
C_LAM = C_SCW + 2 * KS
C_INIT = C_LAM + 4 * DK
C_REST = C_INIT + 1
NPAR = C_REST + 1

K_ID = 0
K_MEAN = K_ID + P
K_DIST = K_MEAN + P
NCONST = K_DIST + TT * T
MASKED = 1e38


class Signals:

    def __init__(self, sem, events):
        self.sem, self.order, self.n, self.next = sem, {e: i for i, e in enumerate(events)}, len(events), 0
        assert len(self.order) == self.n

    def one(self, event):
        assert self.order[event] == self.next % self.n, event
        self.next += 1
        return 1

    def at(self, layer, event):
        return layer * self.n + self.order[event] + 1


def hymba_kernel(nc, x_d, mem_d, memT_d, w_d, par_d, const_d, fin_d, out_d):
    ctx = ExitStack()
    with ctx:
        def sb(name, shape, dt=F32):
            return ctx.enter_context(nc.sbuf_tensor(name, shape, dt))

        def sem(name):
            return ctx.enter_context(nc.semaphore(name))

        def signals(name, events):
            return Signals(sem(name), events)

        w_raw = sb("w_raw", [P, SLOTS, BLOCK])
        w_hi = sb("w_hi", [P, SLOTS, BLOCK], F32R)
        w_lo = sb("w_lo", [P, SLOTS, BLOCK], F32R)
        x = sb("x", [P, TT, D])
        a_hi = sb("a_hi", [P, KD, T], F32R)
        a_lo = sb("a_lo", [P, KD, T], F32R)
        m_hi = sb("m_hi", [P, KD, T], F32R)
        m_lo = sb("m_lo", [P, KD, T], F32R)
        hT_hi = sb("hT_hi", [P, 2, 2, T], F32R)
        hT_lo = sb("hT_lo", [P, 2, 2, T], F32R)
        const = sb("const", [P, NCONST])
        ident = const[:, K_ID:K_ID + P]
        mean_w = const[:, K_MEAN:K_MEAN + P]
        par = sb("par", [P, NPAR])
        half = sb("half", [P, 8])
        over_dv = sb("over_dv", [P, 8])
        eps = sb("eps", [P, 8])
        ssq = sb("ssq", [P, 2, TT])
        var = sb("var", [P, TT])
        rinv = sb("rinv", [P, TT])
        ssm = sb("ssm", [P, TT])
        rmem = sb("rmem", [P, TT])
        junk = sb("junk", [P, D], BF16)
        zqk = sb("zqk", [P, 2, TT, N])
        qkT = sb("qkT", [P, 2 * HEADS, T])
        hq = zqk[:, :, :, :].rearrange("p a t n -> p (a t n)").rearrange("p (t n) -> p t n", t=TT)
        hqT = qkT
        v_sb = sb("v_sb", [P, TT, N])
        u_sb = sb("u_sb", [P, TT, CC])
        gbc = sb("gbc", [P, TT, N])
        gch = sb("gch", [P, TT, CC])
        sig = sb("sig", [P, TT, CC])
        u_pad = sb("u_pad", [P, 2, KC - 1 + T])
        s_pad = sb("s_pad", [P, 2, KS - 1 + T])
        gbT = sb("gbT", [P, 2, T])
        on_sb = sb("on_sb", [P, TT, HEADS, DV])
        acc = sb("acc", [P, 2, T])
        accs = sb("accs", [P, 2, T])
        acc_end = on_sb[:, 1, :, :].rearrange("p h d -> p (h d)").rearrange("p (c t) -> p c t", c=2)
        sq = sig
        std = sb("std", [P, T])
        s_sb = sb("s_sb", [P, 2, T])
        e_sb = sb("e_sb", [P, 2, 2, T])
        prob = sb("prob", [P, T])
        probT = sb("probT", [P, 2, 2, P])
        o_sb = gch[:, :, :].rearrange("p t c -> p (t c)").rearrange("p (h d) -> p h d", h=HEADS)
        sg = sig
        h_sb = u_sb
        kx = sb("kx", [P, TT, D])
        m_raw = kx[:, :, :].rearrange("p t n -> p (t n)").rearrange("p (k m) -> p k m", k=KD)
        vx = sb("vx", [P, TT, D])
        kxT = sb("kxT", [P, KD, T])
        e_x = e_sb[:, :, 0, :]
        o_x = s_sb
        mx = sb("mx", [P, 2])
        nmx = sb("nmx", [P, 2, 2])
        den = sb("den", [P, 2, 2])
        rden = sb("rden", [P, 4])
        sso = sb("sso", [P, TT, HEADS])
        varo = sb("varo", [P, TT, HEADS])
        ro = sb("ro", [P, TT, HEADS])
        lam2 = sb("lam2", [P, 2])
        elam = sb("elam", [P, 2])
        lam = sb("lam", [P, 1])
        gsub = sb("gsub", [P, 1])
        fing = gbc[:, :, :].rearrange("p t n -> p (t n)")
        y = vx

        G = [ctx.enter_context(nc.psum_tensor(f"G{i}", [P, N], F32)) for i in range(4)]
        DB = [ctx.enter_context(nc.psum_tensor(f"D{i}", [P, N], F32)) for i in range(4)]

        s_x = [sem("x_loaded0"), sem("x_loaded1")]
        s_id = sem("identity_loaded")
        s_const = sem("const_loaded")
        s_mem = sem("mem_loaded")
        s_fing = sem("final_gain_loaded")
        s_par = sem("params_loaded")
        s_mraw = sem("memT_loaded")
        s_out = sem("out_stored")
        w_in = [sem(f"w_loaded{i}") for i in range(SLOTS)]
        s_hi = sem("w_hi_ready")
        s_lo = sem("w_lo_ready")
        s_blk = sem("block_multiplied")
        s_init = sem("constants_set")
        s_rmem = sem("rmem_ready")
        s_ssm = sem("ssm_ready")
        s_xup = sem("x_updated")
        s_half = sem("first_half_summed")
        s_xT = sem("xT_in_psum")
        s_ahi = sem("a_hi_ready")
        s_alo = sem("a_lo_ready")
        s_ssq = sem("ssq_ready")
        s_rinv = sem("rinv_ready")
        s_silu = sem("silu_ready")
        s_h = sem("h_ready")
        s_hT = sem("hT_in_psum")
        s_hhi = sem("hT_hi_ready")
        s_hlo = sem("hT_lo_ready")
        s_gained = sem("x_times_final_gain")
        s_fin = [sem("final_ready0"), sem("final_ready1")]
        mm_ = signals("mem_ready", ["hi", "lo"])
        conv_pe = signals("conv_pe", ["uT", "sT", "gbT", "mean", "var"])
        conv_act = signals("conv_act", ["sig", "uT", "gbc", "sT", "gbT", "std", "schi", "cchi"])
        conv_dve = signals("conv_dve", ["u", "gch", "acc", "sq", "sclo", "norm", "cclo"])
        conv_pool = signals("conv_pool", ["acc", "sc"])
        units = range(TT * HEADS)
        att_pe = signals("att_pe", ["qT0", "qT1", "kT0", "kT1", "S0", "S1"] + [
            f"{e}{u + d}" for u in units for e, d in (("pv", -1), ("aT", 0), ("S", 2))
            if 0 <= u + d < len(units) and f"{e}{u + d}" != "pv7"] + ["kx0", "pv7", "oT0", "oT1", "kx1"])
        att_act = signals("att_act", ["q", "qT", "k", "kT", "v", "elam", "exp0"] + [
            e for u in units for e in
            ([f"exp{u + 1}"] if u + 1 < len(units) else []) + ([f"kv{u // 2}"] if u % 2 else [])
            + [f"aT{u}"] + (["o0"] if u == 4 else [])] + ["o1", "kx0", "oT0", "oT1", "kx1"])
        att_dve = signals("att_dve", ["lam2", "max0", "lam"] + [
            e for u in units for e in
            [f"a{u}"] + ([f"max{u + 1}"] if u + 1 < len(units) else []) + (["sso0"] if u == 4 else []) + (["on0"] if u == 5 else [])]
            + ["sso1", "on1", "oT0", "oT1"])
        att_pool = signals("att_pool", ["ro0", "ro1"])
        def steps(*parts):
            return [f"{name}{s + d}" for s in range(10) for name, d in parts if 0 <= s + d < 8]

        xa_pe = signals("xa_pe", ["hqT0", "S0"] + steps(("S", 1), ("pT", 0), ("pv", -1), ("oT", -2)) + ["hqT1"])
        xa_act = signals("xa_act", ["hq0", "hqT0", "exp0", "hq1"] + steps(("pT", 0), ("exp", 1), ("o", -1), ("oT", -2))
                         + ["hqT1"])
        xa_dve = signals("xa_dve", ["max0"] + steps(("rden", 0), ("max", 1), ("oT", -2)))
        for s_, first in ((xa_pe, "S2"), (xa_act, "pT1")):
            order = sorted(s_.order, key=s_.order.get)
            order.remove("hqT1")
            order.insert(order.index(first), "hqT1")
            s_.order = {e: i for i, e in enumerate(order)}

        XA_SPLITS = {4: (B_O + 1, B_O + 2), 6: (B_O + 3,), 8: (B_FFN2,)}
        XA_BLOCKS = {4: 0, 6: 1, 8: 2}

        TAPS_V = 18

        TAPS_V = 18
        SCALE = DK ** -0.5
        XSCALE = XD ** -0.5
        SLOPES = [2.0 ** (-8.0 * (h + 1) / HEADS) for h in range(HEADS)]

        def width(i):
            i %= NB
            return (PIECES[i][1] - PIECES[i][0]) * N if i < len(PIECES) else BLOCK

        def gain(norm, k):
            c = C_GAIN + 8 * NORMS.index(norm) + k
            return par[:, c:c + 1]

        def col(c):
            return par[:, c:c + 1]

        def tok(t):
            return slice(t * P, (t + 1) * P)

        def xT(k):
            bank, c = (G[2], DB[0], DB[2])[k // 2 if k < 4 else 2], (k - 4) // 2 if k > 5 else 0
            if k % 2:
                bank = (G[3], DB[1], DB[3])[k // 2 if k < 4 else 2]
            return bank[:, c * T:(c + 1) * T]

        def kv_banks(ch):
            return G[0:2] if ch % 2 == 0 else DB[2:4]

        block = ctx.enter_context(nc.Block())

        @block.sync
        def _(sp):
            def load(l, i, j=0):
                sp.wait_ge(s_lo, l * NB + j * SLOTS + i + 1)
                sp.dma_start(w_raw[:, i % SLOTS, 0:width(i)],
                             w_d[bass.ds(l * NB + j * SLOTS + i, 1)].rearrange("a p n -> (a p) n")[:, 0:width(i)]
                             ).then_inc(w_in[i % SLOTS], 16)

            for i in range(AHEAD):
                load(0, i)
            with sp.Fori(0, L) as l:
                sp.dma_start(par[:, :], par_d[bass.ds(l, 1)].rearrange("a p n -> (a p) n")).then_inc(s_par, 16)
                for i in range(AHEAD, 3 * SLOTS):
                    load(l, i)
                sp.dma_start(m_raw, memT_d).then_inc(s_mraw, 16)
                sp.dma_start(vx[:, :, :], mem_d.rearrange("(t p) n -> p t n", p=P)).then_inc(s_mem, 16)
                with sp.Fori(0, ROUNDS - 3) as j:
                    for i in range(3 * SLOTS, 4 * SLOTS):
                        load(l, i, j)
                for i in range(NB, NB + AHEAD):
                    load(l, i)
            sp.dma_start(fing, fin_d).then_inc(s_fing, 16)
            for n in range(2):
                for t in reversed(range(TT)):
                    w = slice(n * N, (n + 1) * N)
                    sp.wait_ge(s_fin[t], n + 1)
                    sp.dma_start(out_d[tok(t), w], y[:, t, w]).then_inc(s_out, 16)
            sp.wait_ge(s_out, 2 * 16 * TT)

        @block.gpsimd
        def _(pool):
            def rsqrt(out, mean_sq, v, n):
                nc.gpsimd.tensor_tensor(v, mean_sq, eps[:, 0:n], ALU.add)
                pool.drain()
                return nc.gpsimd.tensor_tensor(out, v, half[:, 0:n], ALU.pow)

            nc.gpsimd.memset(half[:, :], -0.5)
            nc.gpsimd.memset(over_dv[:, :], 1.0 / DV)
            nc.gpsimd.memset(u_pad[:, :, :], 0.0)
            nc.gpsimd.memset(s_pad[:, :, :], 0.0)
            nc.gpsimd.memset(eps[:, :], EPS).then_inc(s_init, 1)
            pool.wait_ge(s_x[0], 16)
            pool.dma_start(x[:, :, N:], x_d[:, N:].rearrange("(t p) n -> p t n", p=P)).then_inc(s_x[1], 16)
            pool.dma_start(const[:, P:], const_d[:, P:]).then_inc(s_const, 16)
            pool.drain()

            def norm(l, phase):
                pool.wait_ge(s_ssq, l * 4 + phase + 1)
                nc.gpsimd.tensor_tensor(var[:, :], ssq[:, 0, :], ssq[:, 1, :], ALU.add)
                pool.drain()
                rsqrt(rinv[:, :], var[:, :], var[:, :], TT).then_inc(s_rinv, 1)

            product = kxT[:, 0:2, :]

            def taps(out, src, weights_at, n, ks, event):
                table = par[:, weights_at:weights_at + 2 * n].rearrange("p (c j) -> p c j", c=2)
                for j in ks:
                    w = table[:, :, j:j + 1].to_broadcast([P, 2, T])
                    last = nc.gpsimd.tensor_tensor(out if j == ks[0] else product, src[:, :, j:j + T], w, ALU.mult)
                    if j != ks[0]:
                        pool.drain()
                        last = nc.gpsimd.tensor_tensor(out, out, product, ALU.add)
                    if event is not None and j == ks[-1]:
                        last.then_inc(conv_pool.sem, conv_pool.one(event))
                    pool.drain()

            with pool.Fori(0, L) as l:
                norm(l, 0)
                pool.drain()
                pool.wait_ge(s_ssm, l + 1)
                rsqrt(rmem[:, :], ssm[:, :], var[:, :], TT).then_inc(s_rmem, 1)
                pool.drain()
                norm(l, 1)
                pool.wait_ge(conv_act.sem, conv_act.at(l, "uT"))
                taps(acc_end, u_pad, C_CCW, KC, range(TAPS_V, KC), "acc")
                pool.wait_ge(conv_act.sem, conv_act.at(l, "gbT"))
                taps(accs[:, :, :], s_pad, C_SCW, KS, range(KS), None)
                nc.gpsimd.tensor_tensor(accs[:, :, :], accs[:, :, :], gbT[:, :, :], ALU.mult
                                        ).then_inc(conv_pool.sem, conv_pool.one("sc"))
                for t in range(TT):
                    pool.wait_ge(att_dve.sem, att_dve.at(l, f"sso{t}"))
                    nc.gpsimd.tensor_tensor(varo[:, t, :], sso[:, t, :], over_dv[:, 0:HEADS], ALU.mult)
                    pool.drain()
                    rsqrt(ro[:, t, :], varo[:, t, :], varo[:, t, :], HEADS
                          ).then_inc(att_pool.sem, att_pool.one(f"ro{t}"))
                norm(l, 2)
                norm(l, 3)
            norm(L, 0)

        @block.scalar
        def _(act):
            A = nc.scalar.activation

            def split(l, i, j=0):
                act.wait_ge(s_blk, l * NB + 2 * SLOTS * j + i + 1)
                s, W = i % SLOTS, width(i)
                act.wait_ge(w_in[s], 16 * (l * ROUNDS + 2 * j + i // SLOTS + 1))
                A(w_hi[:, s, 0:W], w_raw[:, s, 0:W], ACT.Copy).then_inc(s_hi, 1)

            def norm_start(l, phase, splits):
                for k in range(KD):
                    if k in splits:
                        split(l, splits[k])
                    act.wait_ge(s_xT, l * 32 + phase * 8 + k + 1)
                    if k >= 6:
                        act.wait_ge(s_alo, l * 32 + phase * 8 + k - 1)
                    A(a_hi[:, k, :], xT(k), ACT.Copy, scale=gain(NORMS[phase], k)).then_inc(s_ahi, 1)

            def squares(l, phase, n):
                for t in range(TT):
                    act.drain()
                    act.wait_ge(s_xup, FIRST + l * 16 + phase * 4 - 3 + 2 * n + t)
                    last = A(junk[:, 0:N], x[:, t, n * N:(n + 1) * N], ACT.Square, scale=D ** -0.5,
                             accum_out=ssq[:, n, t:t + 1])
                if n == 1:
                    last.then_inc(s_ssq, 1)

            def silu(l, f, j, c):
                act.wait_ge(s_blk, SLOTS + l * NB + (B_FFN1, B_FFN2)[f] + 6 * j + (3 * c + 1 if c else 2))
                for t in range(TT):
                    A(sg[:, t, :], G[2 * (c % 2) + t][:, 0:CF], ACT.Silu, scale=rinv[:, t:t + 1]
                      ).then_inc(s_silu, 1)

            def hidden_hi(l, f, j, c, slot=0):
                act.wait_ge(s_hT, l * 2 * STEPS + f * STEPS + 2 * j + c + 1)
                A(hT_hi[:, slot, :, :], G[2 * (c % 2)][:, :].rearrange("p (k t) -> p k t", k=2), ACT.Copy
                  ).then_inc(s_hhi, 1)

            def memory_hi(l):
                act.wait_ge(s_mraw, 16 * l + 16)
                for k in range(KD):
                    last = A(m_hi[:, k, :], m_raw[:, k, :], ACT.Copy, scale=gain("mem_norm", k))
                last.then_inc(mm_.sem, mm_.one("hi"))
                for t in range(TT):
                    act.drain()
                    if t == 0:
                        act.wait_ge(s_mem, 16 * l + 16)
                    last = A(junk[:, :], vx[:, t, :], ACT.Square, scale=D ** -0.5, accum_out=ssm[:, t:t + 1])
                last.then_inc(s_ssm, 1)

            def ffn(l, f):
                base = (B_FFN1, B_FFN2)[f]
                norm_start(l, 3 * f, {4: base + 2} if f else {2: 2, 4: 3, 6: 4})
                squares(l, 3 * f, 0)
                squares(l, 3 * f, 1)
                act.wait_ge(s_rinv, l * 4 + 3 * f + 1)
                silu(l, f, 0, 0)

                def step(j, c):
                    n = base + 3 * c
                    split(l, n, j)
                    split(l, n + 1, j)
                    hidden_hi(l, f, j, c - 1)
                    split(l, n + 2, j)
                    silu(l, f, j, c)

                step(0, 1)
                with act.Fori(0, PAIRS) as j:
                    step(j, 2)
                    step(j, 3)
                if f == 0:
                    memory_hi(l)
                step(PAIRS, 2)
                split(l, base + FFN_BLOCKS)
                hidden_hi(l, f, PAIRS, 2, slot=1)
                split(l, base + FFN_BLOCKS + 1)

            def mixer(l):
                norm_start(l, 1, {4: B_IN + 2})
                squares(l, 1, 0)
                squares(l, 1, 1)
                act.wait_ge(s_rinv, l * 4 + 2)
                act.wait_ge(s_blk, SLOTS + l * NB + B_IN + 2)
                for t in range(TT):
                    last = A(sig[:, t, :], G[t][:, CC:2 * CC], ACT.Sigmoid, scale=rinv[:, t:t + 1])
                last.then_inc(conv_act.sem, conv_act.one("sig"))
                split(l, B_IN + 3)
                act.wait_ge(conv_pe.sem, conv_pe.at(l, "uT"))
                A(u_pad[:, :, KC - 1:], DB[0][:, :].rearrange("p (c t) -> p c t", c=2), ACT.Copy
                  ).then_inc(conv_act.sem, conv_act.one("uT"))
                split(l, B_IN + 4)
                act.wait_ge(s_blk, SLOTS + l * NB + B_IN + 4)
                for t in range(TT):
                    last = A(gbc[:, t, :], G[2 + t][:, :], ACT.Copy, scale=rinv[:, t:t + 1])
                last.then_inc(conv_act.sem, conv_act.one("gbc"))
                split(l, B_IN + 5)
                split(l, B_IN + 6)
                act.wait_ge(conv_pe.sem, conv_pe.at(l, "sT"))
                A(s_pad[:, :, KS - 1:], DB[1][:, :].rearrange("p (c t) -> p c t", c=2), ACT.Copy
                  ).then_inc(conv_act.sem, conv_act.one("sT"))
                act.wait_ge(conv_pe.sem, conv_pe.at(l, "gbT"))
                A(gbT[:, :, :], DB[2][:, :].rearrange("p (c t) -> p c t", c=2), ACT.Copy
                  ).then_inc(conv_act.sem, conv_act.one("gbT"))
                split(l, B_IN + 7)
                for w, name in enumerate("qk"):
                    act.wait_ge(s_blk, SLOTS + l * NB + B_IN + 7 + 2 * w)
                    for t in range(TT):
                        last = A(zqk[:, w, t, :], G[2 * (1 - w) + t][:, :], ACT.Copy, scale=rinv[:, t:t + 1])
                    last.then_inc(att_act.sem, att_act.one(name))
                    split(l, B_IN + 8 + 2 * w)
                    for b in range(2):
                        act.wait_ge(att_pe.sem, att_pe.at(l, f"{name}T{b}"))
                        last = A(qkT[:, 4 * w + 2 * b:4 * w + 2 * b + 2, :],
                                 DB[(3, 0, 1, 2)[2 * w + b]][:, :].rearrange("p (h t) -> p h t", h=2), ACT.Copy)
                    last.then_inc(att_act.sem, att_act.one(f"{name}T"))
                    split(l, B_IN + 9 + 2 * w)
                split(l, B_KV + 1)
                act.wait_ge(s_blk, SLOTS + l * NB + B_IN + 11)
                for t in range(TT):
                    last = A(v_sb[:, t, :], G[2 + t][:, :], ACT.Copy, scale=rinv[:, t:t + 1])
                last.then_inc(att_act.sem, att_act.one("v"))
                act.wait_ge(att_dve.sem, att_dve.at(l, "lam2"))
                A(elam[:, :], lam2[:, :], ACT.Exp).then_inc(att_act.sem, att_act.one("elam"))
                act.wait_ge(s_rmem, l + 1)

                def exp(u):
                    W = P * (u // HEADS + 1)
                    act.wait_ge(att_dve.sem, att_dve.at(l, f"max{u}"))
                    for c in range(2):
                        last = A(e_sb[:, u % 2, c, 0:W], s_sb[:, c, 0:W], ACT.Exp, scale=SCALE,
                                 bias=nmx[:, u % 2, c:c + 1], accum_out=den[:, u % 2, c:c + 1])
                    last.then_inc(att_act.sem, att_act.one(f"exp{u}"))

                def o_copy(t):
                    act.wait_ge(att_pe.sem, att_pe.at(l, f"pv{HEADS * t + HEADS - 1}"))
                    if t:
                        act.wait_ge(att_dve.sem, att_dve.at(l, "on0"))
                    A(o_sb[:, :, :], G[3][:, :].rearrange("p (h d) -> p h d", h=HEADS), ACT.Copy
                      ).then_inc(att_act.sem, att_act.one(f"o{t}"))

                exp(0)
                for u in units:
                    split(l, B_KV + u + 2)
                    if u == 5:
                        act.wait_ge(conv_pe.sem, conv_pe.at(l, "var"))
                        A(std[:, :], DB[3][:, 0:T], ACT.Sqrt, bias=eps[:, 0:1]).then_inc(conv_act.sem, conv_act.one("std"))
                    if u + 1 < len(units):
                        exp(u + 1)
                    if u == 5:
                        act.wait_ge(conv_pool.sem, conv_pool.at(l, "sc"))
                        A(a_hi[:, A_SC:A_SC + 2, :], accs[:, :, :], ACT.Copy).then_inc(conv_act.sem, conv_act.one("schi"))
                    if u == 7:
                        act.wait_ge(conv_dve.sem, conv_dve.at(l, "norm"))
                        A(sq[:, :, :], acc[:, :, :], ACT.Silu)
                        act.drain()
                        A(a_hi[:, A_CC:A_CC + 2, :], sq[:, :, :], ACT.Copy).then_inc(conv_act.sem, conv_act.one("cchi"))
                    if u % 2:
                        act.wait_ge(s_blk, SLOTS + l * NB + B_KV + u + 1)
                        ch = u // 2
                        for t in range(TT):
                            last = A((kx, vx)[ch // 2][:, t, (ch % 2) * N:(ch % 2 + 1) * N], kv_banks(ch)[t][:, :],
                                     ACT.Copy, scale=rmem[:, t:t + 1])
                        last.then_inc(att_act.sem, att_act.one(f"kv{ch}"))
                    act.wait_ge(att_pe.sem, att_pe.at(l, f"aT{u}"))
                    kt = u // HEADS + 1
                    A(probT[:, 0, 0:kt, :], G[2][:, 0:kt * P].rearrange("p (k t) -> p k t", k=kt), ACT.Copy
                      ).then_inc(att_act.sem, att_act.one(f"aT{u}"))
                    if u == 4:
                        o_copy(0)
                o_copy(1)

                def kx_copy(ch):
                    act.wait_ge(att_pe.sem, att_pe.at(l, f"kx{ch}"))
                    for b in range(2):
                        last = A(kxT[:, 4 * ch + 2 * b:4 * ch + 2 * b + 2, :],
                                 G[b][:, :].rearrange("p (h t) -> p h t", h=2), ACT.Copy)
                    last.then_inc(att_act.sem, att_act.one(f"kx{ch}"))

                def o_hi(t):
                    act.wait_ge(att_pe.sem, att_pe.at(l, f"oT{t}"))
                    A(a_hi[:, A_ATT:, tok(t)], G[2 + t][:, :].rearrange("p (h t) -> p h t", h=HEADS), ACT.Copy,
                      scale=gsub[:, 0:1]).then_inc(att_act.sem, att_act.one(f"oT{t}"))

                split(l, B_OUT + 2)
                kx_copy(0)
                o_hi(0)
                split(l, B_OUT + 3)
                o_hi(1)
                split(l, B_Q)
                kx_copy(1)
                split(l, B_Q + 1)

            def cross(l):
                norm_start(l, 2, {4: B_Q + 2})
                squares(l, 2, 0)
                squares(l, 2, 1)
                act.wait_ge(s_rinv, l * 4 + 3)

                def hq_copy(ch):
                    act.wait_ge(s_blk, SLOTS + l * NB + B_Q + 2 * ch + 2)
                    for t in range(TT):
                        last = A(hq[:, t, ch * N:(ch + 1) * N], G[2 * ch + t][:, :], ACT.Copy,
                                 scale=rinv[:, t:t + 1])
                    last.then_inc(xa_act.sem, xa_act.one(f"hq{ch}"))

                def hqT_copy(ch):
                    act.wait_ge(xa_pe.sem, xa_pe.at(l, f"hqT{ch}"))
                    for b in range(2):
                        last = A(hqT[:, 4 * ch + 2 * b:4 * ch + 2 * b + 2, :],
                                 DB[2 * ch + b][:, :].rearrange("p (h t) -> p h t", h=2), ACT.Copy)
                    last.then_inc(xa_act.sem, xa_act.one(f"hqT{ch}"))

                def exp(u):
                    act.wait_ge(xa_dve.sem, xa_dve.at(l, f"max{u}"))
                    A(e_x[:, u % 2, :], G[0][:, 0:T], ACT.Exp, scale=XSCALE, bias=nmx[:, u % 2, 0:1],
                      accum_out=den[:, u % 2, 0:1]).then_inc(xa_act.sem, xa_act.one(f"exp{u}"))

                def oT_hi(u):
                    h, t = u // 2, u % 2
                    act.wait_ge(xa_pe.sem, xa_pe.at(l, f"oT{u}"))
                    A(a_hi[:, 2 * h:2 * h + 2, tok(t)], G[3][:, 0:T].rearrange("p (k t) -> p k t", k=2),
                      ACT.Copy).then_inc(xa_act.sem, xa_act.one(f"oT{u}"))

                def probT_copy(u):
                    act.wait_ge(xa_pe.sem, xa_pe.at(l, f"pT{u}"))
                    A(probT[:, u % 2, :, :], G[1][:, 0:T].rearrange("p (k t) -> p k t", k=2), ACT.Copy
                      ).then_inc(xa_act.sem, xa_act.one(f"pT{u}"))

                def o_copy(u):
                    act.wait_ge(xa_dve.sem, xa_dve.at(l, f"rden{u}"))
                    act.wait_ge(xa_pe.sem, xa_pe.at(l, f"pv{u}"))
                    A(o_x[:, u % 2, :], G[2][:, 0:T], ACT.Copy, scale=rden[:, u % 4:u % 4 + 1]
                      ).then_inc(xa_act.sem, xa_act.one(f"o{u}"))

                split(l, B_Q + 3)
                hq_copy(0)
                split(l, B_O)
                hqT_copy(0)
                exp(0)
                hq_copy(1)
                for u in range(10):
                    if u == 1:
                        hqT_copy(1)
                    if u < 8:
                        probT_copy(u)
                    if u < 7:
                        exp(u + 1)
                    if 1 <= u < 9:
                        o_copy(u - 1)
                    if u >= 2:
                        oT_hi(u - 2)
                    for i in XA_SPLITS.get(u, ()):
                        split(l, i)
                split(l, B_FFN2 + 1)

            act.dma_start(const[:, 0:P], const_d[:, 0:P]).then_inc(s_id, 16)
            act.dma_start(x[:, :, 0:N], x_d[:, 0:N].rearrange("(t p) n -> p t n", p=P)).then_inc(s_x[0], 16)
            act.wait_ge(s_init, 1)
            with act.Fori(0, L) as l:
                act.wait_ge(s_par, 16 * l + 16)
                ffn(l, 0)
                mixer(l)
                cross(l)
                ffn(l, 1)
            squares(L, 0, 0)
            squares(L, 0, 1)
            act.wait_ge(s_gained, 1)
            act.wait_ge(s_rinv, 4 * L + 1)
            for n in range(2):
                w = slice(n * N, (n + 1) * N)
                A(y[:, 0, w], y[:, 0, w], ACT.Copy, scale=rinv[:, 0:1]).then_inc(s_fin[0], 1)

        @block.vector
        def _(dve):
            V = nc.vector

            def split(l, i, j=0):
                dve.wait_ge(s_hi, l * NB + 2 * SLOTS * j + i + 1)
                s, W = i % SLOTS, width(i)
                V.tensor_tensor(w_lo[:, s, 0:W], w_raw[:, s, 0:W], w_hi[:, s, 0:W].bitcast(F32), ALU.subtract
                                ).then_inc(s_lo, 1)

            def a_lo_part(l, phase, ks):
                for k in ks:
                    dve.wait_ge(s_ahi, l * 32 + phase * 8 + k + 1)
                    V.scalar_tensor_tensor(a_lo[:, k, :], xT(k), gain(NORMS[phase], k),
                                           a_hi[:, k, :].bitcast(F32), ALU.mult, ALU.subtract).then_inc(s_alo, 1)

            def x_update(n, factor):
                for t in range(TT):
                    xs = x[:, t, n * N:(n + 1) * N]
                    V.scalar_tensor_tensor(xs, DB[2 * n + t][:, :], factor, xs, ALU.mult, ALU.add
                                           ).then_inc(s_xup, 1)

            def first_half(l, phase, factor):
                dve.wait_ge(s_half, l * 4 + phase + 1)
                x_update(0, factor)

            def second_half(l, phase, last_block, factor, i):
                a_lo_part(l, phase + 1, range(0, 2))
                dve.wait_ge(s_blk, SLOTS + l * NB + last_block + 1)
                x_update(1, factor)
                a_lo_part(l, phase + 1, range(2, 8))
                split(l, i)

            def hidden(l, f, j, c):
                dve.wait_ge(s_rinv, l * 4 + 3 * f + 1)
                for t in range(TT):
                    dve.wait_ge(s_silu, l * 4 * STEPS + f * 2 * STEPS + 4 * j + 2 * c + t + 1)
                    V.scalar_tensor_tensor(h_sb[:, t, :], G[2 * (c % 2) + t][:, CF:2 * CF], rinv[:, t:t + 1],
                                           sg[:, t, :], ALU.mult, ALU.mult).then_inc(s_h, 1)

            def hidden_lo(l, f, j, c, slot=0):
                dve.wait_ge(s_hhi, l * 2 * STEPS + f * STEPS + 2 * j + c + 1)
                V.tensor_tensor(hT_lo[:, slot, :, :], G[2 * (c % 2)][:, :].rearrange("p (k t) -> p k t", k=2),
                                hT_hi[:, slot, :, :].bitcast(F32), ALU.subtract).then_inc(s_hlo, 1)

            def ffn(l, f):
                base = (B_FFN1, B_FFN2)[f]
                if f == 0:
                    for k in range(KD):
                        if k in (2, 4, 6):
                            split(l, {2: 2, 4: 3, 6: 4}[k])
                        a_lo_part(l, 0, [k])
                hidden(l, f, 0, 0)

                def step(j, c):
                    n = base + 3 * c
                    split(l, n, j)
                    split(l, n + 1, j)
                    hidden_lo(l, f, j, c - 1)
                    split(l, n + 2, j)
                    hidden(l, f, j, c)

                step(0, 1)
                with dve.Fori(0, PAIRS) as j:
                    step(j, 2)
                    step(j, 3)
                if f == 0:
                    dve.wait_ge(mm_.sem, mm_.at(l, "hi"))
                    for k in range(KD):
                        last = V.scalar_tensor_tensor(m_lo[:, k, :], m_raw[:, k, :], gain("mem_norm", k),
                                                      m_hi[:, k, :].bitcast(F32), ALU.mult, ALU.subtract)
                    last.then_inc(mm_.sem, mm_.one("lo"))
                step(PAIRS, 2)
                split(l, base + FFN_BLOCKS)
                hidden_lo(l, f, PAIRS, 2, slot=1)
                first_half(l, 3 * f, 0.5)
                split(l, base + FFN_BLOCKS + 1)
                if f == 0:
                    second_half(l, 0, B_IN - 1, 0.5, B_IN + 2)
                else:
                    dve.wait_ge(s_blk, SLOTS + l * NB + NB)
                    x_update(1, 0.5)

            def mixer(l):
                for i in range(2):
                    q, k = C_LAM + 2 * i * DK, C_LAM + (2 * i + 1) * DK
                    last = V.scalar_tensor_tensor(lamj[:, i, :], par[:, q:q + DK], 1.0, par[:, k:k + DK],
                                                  ALU.mult, ALU.mult, accum_out=lam2[:, i:i + 1])
                last.then_inc(att_dve.sem, att_dve.one("lam2"))
                V.tensor_scalar(gsub[:, :], col(C_SUB), col(C_REST), None, ALU.mult)
                dve.wait_ge(s_rinv, l * 4 + 2)
                dve.wait_ge(conv_act.sem, conv_act.at(l, "sig"))
                for t in range(TT):
                    last = V.scalar_tensor_tensor(u_sb[:, t, :], G[t][:, 0:CC], rinv[:, t:t + 1], sig[:, t, :],
                                                  ALU.mult, ALU.mult)
                last.then_inc(conv_dve.sem, conv_dve.one("u"))
                split(l, B_IN + 3)

                def taps(ks):
                    for j in ks:
                        for c in range(2):
                            w = col(C_CCW + c * KC + j)
                            src = u_pad[:, c, j:j + T]
                            if j == 0:
                                V.tensor_scalar(acc[:, c, :], src, w, col(C_CCB + c), ALU.mult, ALU.add)
                            else:
                                V.scalar_tensor_tensor(acc[:, c, :], src, w, acc[:, c, :], ALU.mult, ALU.add)
                        dve.drain()

                split(l, B_IN + 4)
                dve.wait_ge(conv_act.sem, conv_act.at(l, "uT"))
                taps(range(0, 3))
                split(l, B_IN + 5)
                taps(range(3, 6))
                dve.wait_ge(conv_act.sem, conv_act.at(l, "gbc"))
                dve.wait_ge(s_blk, SLOTS + l * NB + B_IN + 5)
                for t in range(TT):
                    last = V.scalar_tensor_tensor(gch[:, t, :], G[t][:, 0:CC], rinv[:, t:t + 1],
                                                  gbc[:, t, CC:2 * CC], ALU.mult, ALU.mult)
                last.then_inc(conv_dve.sem, conv_dve.one("gch"))
                split(l, B_IN + 6)
                taps(range(6, 8))
                for n in range(4):
                    split(l, B_IN + 7 + n)
                    taps(range(8 + 2 * n, 10 + 2 * n))
                split(l, B_KV)

                def scores(u):
                    t, h = u // HEADS, u % HEADS
                    W = P * (t + 1)
                    dve.wait_ge(att_pe.sem, att_pe.at(l, f"S{u}"))
                    if u:
                        dve.wait_ge(att_act.sem, att_act.at(l, f"exp{u - 1}"))
                    dist = const[:, K_DIST + t * T:K_DIST + t * T + W]
                    for c in range(2):
                        V.scalar_tensor_tensor(s_sb[:, c, 0:W], dist, -SLOPES[h] / SCALE, DB[c][:, 0:W],
                                               ALU.mult, ALU.add)
                    dve.drain()
                    V.reduce_max(mx[:, :], s_sb[:, :, 0:W], AX_X)
                    dve.drain()
                    V.tensor_scalar(nmx[:, u % 2, :], mx[:, :], -SCALE, None, ALU.mult
                                    ).then_inc(att_dve.sem, att_dve.one(f"max{u}"))

                def combine(u):
                    W = P * (u // HEADS + 1)
                    dve.wait_ge(att_act.sem, att_act.at(l, f"exp{u}"))
                    V.reciprocal(rden[:, 0:2], den[:, u % 2, :])
                    dve.drain()
                    V.tensor_scalar(rden[:, 1:2], rden[:, 1:2], lam[:, 0:1], None, ALU.mult)
                    dve.drain()
                    V.tensor_scalar(e_sb[:, u % 2, 1, 0:W], e_sb[:, u % 2, 1, 0:W], rden[:, 1:2], None, ALU.mult)
                    dve.drain()
                    if u:
                        dve.wait_ge(att_pe.sem, att_pe.at(l, f"aT{u - 1}"))
                    V.scalar_tensor_tensor(prob[:, 0:W], e_sb[:, u % 2, 0, 0:W], rden[:, 0:1],
                                           e_sb[:, u % 2, 1, 0:W], ALU.mult, ALU.subtract
                                           ).then_inc(att_dve.sem, att_dve.one(f"a{u}"))

                def o_squares(t):
                    dve.wait_ge(att_act.sem, att_act.at(l, f"o{t}"))
                    for h in range(HEADS):
                        last = V.scalar_tensor_tensor(on_sb[:, t, h, :], o_sb[:, h, :], 1.0, o_sb[:, h, :],
                                                      ALU.mult, ALU.mult, accum_out=sso[:, t, h:h + 1])
                    last.then_inc(att_dve.sem, att_dve.one(f"sso{t}"))

                def o_norm(t):
                    dve.wait_ge(att_pool.sem, att_pool.at(l, f"ro{t}"))
                    for h in range(HEADS):
                        last = V.tensor_scalar(on_sb[:, t, h, :], o_sb[:, h, :], ro[:, t, h:h + 1], None, ALU.mult)
                    last.then_inc(att_dve.sem, att_dve.one(f"on{t}"))

                scores(0)
                split(l, B_KV + 1)
                dve.wait_ge(att_act.sem, att_act.at(l, "elam"))
                V.scalar_tensor_tensor(lam[:, :], elam[:, 0:1], col(C_INIT), elam[:, 1:2], ALU.add, ALU.subtract
                                       ).then_inc(att_dve.sem, att_dve.one("lam"))
                for u in units:
                    combine(u)
                    if u + 1 < len(units):
                        scores(u + 1)
                    if u < TAPS_V - 16:
                        taps([16 + u])
                    if u == 3:
                        dve.wait_ge(conv_pool.sem, conv_pool.at(l, "acc"))
                        V.tensor_tensor(acc[:, :, :], acc[:, :, :], acc_end, ALU.add
                                        ).then_inc(conv_dve.sem, conv_dve.one("acc"))
                        dve.drain()
                    if u == 4:
                        dve.wait_ge(conv_pe.sem, conv_pe.at(l, "mean"))
                        for c in range(2):
                            V.tensor_tensor(acc[:, c, :], acc[:, c, :], DB[2][:, 0:T], ALU.subtract)
                        dve.drain()
                        V.tensor_tensor(sq[:, :, :], acc[:, :, :], acc[:, :, :], ALU.mult
                                        ).then_inc(conv_dve.sem, conv_dve.one("sq"))
                    split(l, B_KV + u + 2)
                    if u == 4:
                        o_squares(0)
                    if u == 5:
                        o_norm(0)
                        dve.wait_ge(conv_act.sem, conv_act.at(l, "schi"))
                        V.tensor_tensor(a_lo[:, A_SC:A_SC + 2, :], accs[:, :, :],
                                        a_hi[:, A_SC:A_SC + 2, :].bitcast(F32), ALU.subtract
                                        ).then_inc(conv_dve.sem, conv_dve.one("sclo"))
                    if u == 6:
                        dve.wait_ge(conv_act.sem, conv_act.at(l, "std"))
                        V.reciprocal(std[:, :], std[:, :])
                        dve.drain()
                        for c in range(2):
                            V.tensor_tensor(acc[:, c, :], acc[:, c, :], std[:, :], ALU.mult)
                        dve.drain()
                        for c in range(2):
                            last = V.tensor_scalar(acc[:, c, :], acc[:, c, :], col(C_LNG + c), col(C_LNB + c),
                                                   ALU.mult, ALU.add)
                        last.then_inc(conv_dve.sem, conv_dve.one("norm"))
                dve.wait_ge(conv_act.sem, conv_act.at(l, "cchi"))
                V.tensor_tensor(a_lo[:, A_CC:A_CC + 2, :], sq[:, :, :],
                                a_hi[:, A_CC:A_CC + 2, :].bitcast(F32), ALU.subtract
                                ).then_inc(conv_dve.sem, conv_dve.one("cclo"))

                def o_lo(t):
                    dve.wait_ge(att_act.sem, att_act.at(l, f"oT{t}"))
                    V.scalar_tensor_tensor(a_lo[:, A_ATT:, tok(t)], G[2 + t][:, :].rearrange("p (h t) -> p h t", h=HEADS),
                                           gsub[:, 0:1], a_hi[:, A_ATT:, tok(t)].bitcast(F32), ALU.mult, ALU.subtract
                                           ).then_inc(att_dve.sem, att_dve.one(f"oT{t}"))

                o_squares(1)
                split(l, B_OUT + 2)
                o_norm(1)
                o_lo(0)
                split(l, B_OUT + 3)
                o_lo(1)
                split(l, B_Q)
                first_half(l, 1, 1.0)
                split(l, B_Q + 1)
                second_half(l, 1, B_OUT + 3, 1.0, B_Q + 2)

            def cross(l):
                split(l, B_Q + 3)
                split(l, B_O)

                def row_max(u):
                    dve.wait_ge(xa_pe.sem, xa_pe.at(l, f"S{u}"))
                    V.reduce_max(mx[:, u % 2:u % 2 + 1], G[0][:, 0:T], AX_X)
                    dve.drain()
                    V.tensor_scalar(nmx[:, u % 2, 0:1], mx[:, u % 2:u % 2 + 1], -XSCALE, None, ALU.mult
                                    ).then_inc(xa_dve.sem, xa_dve.one(f"max{u}"))

                def oT_lo(u):
                    h, t = u // 2, u % 2
                    dve.wait_ge(xa_act.sem, xa_act.at(l, f"oT{u}"))
                    V.tensor_tensor(a_lo[:, 2 * h:2 * h + 2, tok(t)],
                                    G[3][:, 0:T].rearrange("p (k t) -> p k t", k=2),
                                    a_hi[:, 2 * h:2 * h + 2, tok(t)].bitcast(F32), ALU.subtract
                                    ).then_inc(xa_dve.sem, xa_dve.one(f"oT{u}"))

                row_max(0)
                for u in range(10):
                    if u < 8:
                        dve.wait_ge(xa_act.sem, xa_act.at(l, f"exp{u}"))
                        V.reciprocal(rden[:, u % 4:u % 4 + 1], den[:, u % 2, 0:1]
                                     ).then_inc(xa_dve.sem, xa_dve.one(f"rden{u}"))
                    if u < 7:
                        row_max(u + 1)
                    if u >= 2:
                        oT_lo(u - 2)
                    for i in XA_SPLITS.get(u, ()):
                        split(l, i)
                first_half(l, 2, 1.0)
                split(l, B_FFN2 + 1)
                second_half(l, 2, B_O + 3, 1.0, B_FFN2 + 2)

            lamj = v_sb[:, 0, 0:2 * DK].rearrange("p (a k) -> p a k", a=2)
            dve.sem_inc(s_lo, SLOTS)
            dve.sem_inc(s_xup, FIRST)
            dve.wait_ge(s_init, 1)
            for i in range(AHEAD):
                dve.wait_ge(w_in[i], 16)
                V.tensor_copy(w_hi[:, i, 0:width(i)], w_raw[:, i, 0:width(i)]).then_inc(s_hi, 1)
                dve.drain()
                split(0, i)
            with dve.Fori(0, L) as l:
                dve.wait_ge(s_par, 16 * l + 16)
                ffn(l, 0)
                mixer(l)
                cross(l)
                ffn(l, 1)
            dve.wait_ge(s_fing, 16)
            dve.drain()
            for t in range(TT):
                V.tensor_tensor(y[:, t, :], x[:, t, :], fing, ALU.mult).then_inc(s_gained, 1)
            dve.drain()
            dve.wait_ge(s_rinv, 4 * L + 1)
            for n in range(2):
                w = slice(n * N, (n + 1) * N)
                V.tensor_scalar(y[:, 1, w], y[:, 1, w], rinv[:, 1:2], None, ALU.mult).then_inc(s_fin[1], 1)

        @block.tensor
        def _(pe):
            M = nc.tensor.matmul
            TR = nc.tensor.transpose

            def weights(l, i, j=0):
                pe.wait_ge(s_lo, SLOTS + l * NB + 2 * SLOTS * j + i + 1)
                return w_hi[:, i % SLOTS, :], w_lo[:, i % SLOTS, :]

            def product(out, hi, lo, whi, wlo, start, stop):
                M(out, hi, whi, start=start, stop=False)
                M(out, hi, wlo, start=False, stop=False)
                return M(out, lo, whi, start=False, stop=stop)

            def wide(l, i, ahi, alo, banks, ks, cols=N, j=0, ready=None, between=None):
                whi, wlo = weights(l, i, j)
                for n, k in enumerate(ks):
                    if n == 2 and between is not None:
                        between()
                    if ready is not None:
                        pe.wait_ge(s_alo, ready + k + 1)
                    for t in range(TT):
                        last = product(banks[t][:, 0:cols], ahi[:, k, tok(t)], alo[:, k, tok(t)],
                                       whi[:, n * cols:(n + 1) * cols], wlo[:, n * cols:(n + 1) * cols],
                                       k == 0, k == KD - 1)
                last.then_inc(s_blk, 1)

            def down(l, i, hi, lo, ks, start, stop, j=0, between=None, near_end=None):
                whi, wlo = weights(l, i, j)
                for n, k in enumerate(ks):
                    if n == 1 and between is not None:
                        between()
                    for c in range(2):
                        w = slice(n * D + c * N, n * D + (c + 1) * N)
                        if (n, c) == (1, 1) and near_end is not None:
                            near_end()
                        for t in range(TT):
                            last = product(DB[2 * c + t][:, :], hi[:, k, tok(t)], lo[:, k, tok(t)], whi[:, w],
                                           wlo[:, w], start and n == 0, stop and n == 1)
                last.then_inc(s_blk, 1)

            def last_down(l, i, hi, lo, ks, phase):
                whi, wlo = weights(l, i)
                for c in range(2):
                    for n, k in enumerate(ks):
                        w = slice(n * D + c * N, n * D + (c + 1) * N)
                        for t in range(TT):
                            if (c, n, t) == (1, 1, 1):
                                pe.wait_ge(s_xup, FIRST + l * 16 + phase * 4 + 2)
                                x_transposes(range(4))
                            last = product(DB[2 * c + t][:, :], hi[:, k, tok(t)], lo[:, k, tok(t)], whi[:, w],
                                           wlo[:, w], False, n == 1)
                    if c == 0:
                        last.then_inc(s_half, 1)
                last.then_inc(s_blk, 1)

            def x_transposes(ks):
                for k in ks:
                    for t in range(TT):
                        last = TR(xT(k)[:, tok(t)], x[:, t, k * P:(k + 1) * P], ident)
                    if k < 4:
                        last.then_inc(s_xT, 1)
                if ks[-1] == 7:
                    last.then_inc(s_xT, 4)

            def first_blocks(l, i, phase):
                def second_half():
                    if i == B_FFN1:
                        pe.wait_ge(s_x[1], 16)
                    pe.wait_ge(s_xup, FIRST + l * 16 + phase * 4)
                    x_transposes(range(4, 8))

                ready = l * 32 + phase * 8
                if i == B_FFN1:
                    for p, ks in enumerate(PIECES):
                        if p == 2:
                            second_half()
                        wide(l, p, a_hi, a_lo, G[0:2], range(*ks), ready=ready)
                else:
                    wide(l, i, a_hi, a_lo, G[0:2], range(4), ready=ready, between=second_half)
                wide(l, i + 1, a_hi, a_lo, G[0:2], range(4, 8), ready=ready)

            def transpose_pairs(src, banks, signals_, names):
                for b, bank in enumerate(banks):
                    for i in range(2):
                        for t in range(TT):
                            last = TR(bank[:, i * T + t * P:i * T + (t + 1) * P], src(t, 2 * b + i), ident)
                    if names[b]:
                        last.then_inc(signals_.sem, signals_.one(names[b]))

            def ffn(l, f):
                base = (B_FFN1, B_FFN2)[f]
                first_blocks(l, base, 3 * f)
                if f == 0:
                    pe.wait_ge(s_const, 16)

                def transposes(j, c):
                    pe.wait_ge(s_h, l * 4 * STEPS + f * 2 * STEPS + 4 * j + 2 * c + 2)
                    for k in range(2):
                        for t in range(TT):
                            last = TR(G[2 * (c % 2)][:, k * T + t * P:k * T + (t + 1) * P],
                                      h_sb[:, t, k * P:(k + 1) * P], ident)
                    last.then_inc(s_hT, 1)

                def hidden_ready(j, c):
                    pe.wait_ge(s_hlo, l * 2 * STEPS + f * STEPS + 2 * j + c + 1)

                def step(j, c, near_end=None, first=False):
                    n = base + 3 * c
                    banks = G[2 * (c % 2):2 * (c % 2) + 2]
                    wide(l, n - 1, a_hi, a_lo, banks, range(4), j=j)
                    transposes(j, c - 1)
                    wide(l, n, a_hi, a_lo, banks, range(4, 8), j=j)
                    hidden_ready(j, c - 1)
                    down(l, n + 1, hT_hi[:, 0], hT_lo[:, 0], range(2), first, False, j=j, near_end=near_end)

                step(0, 1, first=True)
                with pe.Fori(0, PAIRS) as j:
                    step(j, 2)
                    step(j, 3)
                step(PAIRS, 2, near_end=lambda: transposes(PAIRS, 2))
                hidden_ready(PAIRS, 2)
                last_down(l, base + FFN_BLOCKS - 1, hT_hi[:, 1], hT_lo[:, 1], range(2), 3 * f)

            def mixer(l):
                first_blocks(l, B_IN, 1)
                wide(l, B_IN + 2, a_hi, a_lo, G[2:4], range(4))
                pe.wait_ge(conv_dve.sem, conv_dve.at(l, "u"))
                transpose_pairs(lambda t, i: u_sb[:, t, i * P:(i + 1) * P], [DB[0]], conv_pe, ["uT"])
                wide(l, B_IN + 3, a_hi, a_lo, G[2:4], range(4, 8))
                wide(l, B_IN + 4, a_hi, a_lo, G[0:2], range(8), cols=CC)
                pe.wait_ge(conv_act.sem, conv_act.at(l, "gbc"))
                wide(l, B_IN + 5, a_hi, a_lo, G[2:4], range(4))
                pe.wait_ge(conv_dve.sem, conv_dve.at(l, "gch"))
                transpose_pairs(lambda t, i: gch[:, t, i * P:(i + 1) * P], [DB[1]], conv_pe, ["sT"])
                transpose_pairs(lambda t, i: gbc[:, t, i * P:(i + 1) * P], [DB[2]], conv_pe, ["gbT"])
                wide(l, B_IN + 6, a_hi, a_lo, G[2:4], range(4, 8))
                wide(l, B_IN + 7, a_hi, a_lo, G[0:2], range(4))
                pe.wait_ge(att_act.sem, att_act.at(l, "q"))
                transpose_pairs(lambda t, i: zqk[:, 0, t, i * P:(i + 1) * P], [DB[3], DB[0]], att_pe, ["qT0", "qT1"])
                wide(l, B_IN + 8, a_hi, a_lo, G[0:2], range(4, 8))
                wide(l, B_IN + 9, a_hi, a_lo, G[2:4], range(4))
                pe.wait_ge(conv_act.sem, conv_act.at(l, "gbT"))
                pe.wait_ge(att_act.sem, att_act.at(l, "k"))
                transpose_pairs(lambda t, i: zqk[:, 1, t, i * P:(i + 1) * P], [DB[1], DB[2]], att_pe, ["kT0", "kT1"])
                wide(l, B_IN + 10, a_hi, a_lo, G[2:4], range(4, 8))

                def S(u):
                    t, h = u // HEADS, u % HEADS
                    W = P * (t + 1)
                    if u:
                        pe.wait_ge(att_dve.sem, att_dve.at(l, f"max{u - 1}"))
                    for c in range(2):
                        r = slice(c * DK, (c + 1) * DK)
                        last = M(DB[c][:, 0:W], qkT[r, h, tok(t)], qkT[r, HEADS + h, 0:W], start=True, stop=True)
                    last.then_inc(att_pe.sem, att_pe.one(f"S{u}"))

                def aT(u):
                    pe.wait_ge(att_dve.sem, att_dve.at(l, f"a{u}"))
                    for k in range(u // HEADS + 1):
                        last = TR(G[2][:, k * P:(k + 1) * P], prob[:, k * P:(k + 1) * P], ident)
                    last.then_inc(att_pe.sem, att_pe.one(f"aT{u}"))

                def pv(u):
                    t, h = u // HEADS, u % HEADS
                    pe.wait_ge(att_act.sem, att_act.at(l, f"aT{u}"))
                    if u == HEADS:
                        pe.wait_ge(att_act.sem, att_act.at(l, "o0"))
                    for k in range(t + 1):
                        last = M(G[3][:, h * DV:(h + 1) * DV], probT[:, 0, k, :], v_sb[:, k, h * DV:(h + 1) * DV],
                                 start=(k == 0), stop=(k == t))
                    last.then_inc(att_pe.sem, att_pe.one(f"pv{u}"))

                pe.wait_ge(att_act.sem, att_act.at(l, "kT"))
                S(0)
                pe.wait_ge(mm_.sem, mm_.at(l, "lo"))
                def moment(event, src, bank):
                    if event == "mean":
                        pe.wait_ge(att_act.sem, att_act.at(l, "kv1"))
                    pe.wait_ge(conv_dve.sem, conv_dve.at(l, {"mean": "acc", "var": "sq"}[event]))
                    for c in range(2):
                        last = M(bank[:, 0:T], mean_w, src[:, c, :], start=(c == 0), stop=(c == 1))
                    last.then_inc(conv_pe.sem, conv_pe.one(event))

                BETWEEN = {0: lambda: S(1), 4: lambda: moment("mean", acc, DB[2])}
                for u in units:
                    if u in (4, 6):
                        pe.wait_ge(att_act.sem, att_act.at(l, f"kv{u // 2 - 2}"))
                    if u == 6:
                        pe.wait_ge(conv_act.sem, conv_act.at(l, "std"))
                    wide(l, B_KV + u, m_hi, m_lo, kv_banks(u // 2), range(4 * (u % 2), 4 * (u % 2) + 4),
                         between=BETWEEN.get(u))
                    if u:
                        pv(u - 1)
                    if u == 0:
                        pe.wait_ge(att_act.sem, att_act.at(l, "v"))
                    aT(u)
                    if u + 2 < len(units):
                        S(u + 2)
                    if u == 4:
                        moment("var", sq, DB[3])

                def out(i, between=None):
                    k = 2 * A_PAIR[i]
                    down(l, B_OUT + i, a_hi, a_lo, (k, k + 1), i == 0, False, between=between)

                def kx_transposes(ch):
                    transpose_pairs(lambda t, i: kx[:, t, (4 * ch + i) * P:(4 * ch + i + 1) * P], [G[0], G[1]],
                                    att_pe, [None, f"kx{ch}"])

                def o_transposes(t):
                    pe.wait_ge(att_dve.sem, att_dve.at(l, f"on{t}"))
                    for h in range(HEADS):
                        last = TR(G[2 + t][:, h * P:(h + 1) * P], on_sb[:, t, h, :], ident)
                    last.then_inc(att_pe.sem, att_pe.one(f"oT{t}"))

                pe.wait_ge(att_act.sem, att_act.at(l, "kv2"))
                kx_transposes(0)
                pe.wait_ge(conv_dve.sem, conv_dve.at(l, "sclo"))
                pe.wait_ge(att_act.sem, att_act.at(l, "kv3"))
                out(0, between=lambda: pv(7))
                o_transposes(0)
                pe.wait_ge(conv_dve.sem, conv_dve.at(l, "cclo"))
                out(1, between=lambda: o_transposes(1))
                pe.wait_ge(att_act.sem, att_act.at(l, "kx0"))
                kx_transposes(1)
                pe.wait_ge(att_dve.sem, att_dve.at(l, "oT1"))
                out(2)
                k = 2 * A_PAIR[3]
                last_down(l, B_OUT + 3, a_hi, a_lo, (k, k + 1), 1)

            def cross(l):
                pe.wait_ge(att_act.sem, att_act.at(l, "kx1"))
                first_blocks(l, B_Q, 2)
                wide(l, B_Q + 2, a_hi, a_lo, G[2:4], range(4))

                def hq_transposes(ch):
                    pe.wait_ge(xa_act.sem, xa_act.at(l, f"hq{ch}"))
                    transpose_pairs(lambda t, i: hq[:, t, (4 * ch + i) * P:(4 * ch + i + 1) * P],
                                    [DB[2 * ch], DB[2 * ch + 1]], xa_pe, [None, f"hqT{ch}"])

                def S(u):
                    h, t = u // 2, u % 2
                    if u == 0:
                        pe.wait_ge(xa_act.sem, xa_act.at(l, "hqT0"))
                    else:
                        pe.wait_ge(xa_act.sem, xa_act.at(l, f"exp{u - 1}"))
                    if u == 4:
                        pe.wait_ge(xa_act.sem, xa_act.at(l, "hqT1"))
                    for k in range(2):
                        last = M(G[0][:, 0:T], hqT[:, 2 * h + k, tok(t)], kxT[:, 2 * h + k, :],
                                 start=(k == 0), stop=(k == 1))
                    last.then_inc(xa_pe.sem, xa_pe.one(f"S{u}"))

                def pT(u):
                    pe.wait_ge(xa_act.sem, xa_act.at(l, f"exp{u}"))
                    if u:
                        pe.wait_ge(xa_act.sem, xa_act.at(l, f"pT{u - 1}"))
                    for k in range(2):
                        last = TR(G[1][:, k * P:(k + 1) * P], e_x[:, u % 2, k * P:(k + 1) * P], ident)
                    last.then_inc(xa_pe.sem, xa_pe.one(f"pT{u}"))

                def pv(u):
                    pe.wait_ge(xa_act.sem, xa_act.at(l, f"pT{u}"))
                    if u:
                        pe.wait_ge(xa_act.sem, xa_act.at(l, f"o{u - 1}"))
                    for k in range(2):
                        last = M(G[2][:, 0:XD], probT[:, u % 2, k, :], vx[:, k, (u // 2) * XD:(u // 2 + 1) * XD],
                                 start=(k == 0), stop=(k == 1))
                    last.then_inc(xa_pe.sem, xa_pe.one(f"pv{u}"))

                def oT(u):
                    pe.wait_ge(xa_act.sem, xa_act.at(l, f"o{u}"))
                    if u:
                        pe.wait_ge(xa_dve.sem, xa_dve.at(l, f"oT{u - 1}"))
                    for k in range(2):
                        last = TR(G[3][:, k * P:(k + 1) * P], o_x[:, u % 2, k * P:(k + 1) * P], ident)
                    last.then_inc(xa_pe.sem, xa_pe.one(f"oT{u}"))

                hq_transposes(0)
                wide(l, B_Q + 3, a_hi, a_lo, G[2:4], range(4, 8), between=lambda: S(0))
                for u in range(10):
                    if u == 1:
                        hq_transposes(1)
                    if u < 7:
                        S(u + 1)
                    if u < 8:
                        pT(u)
                    if 1 <= u < 9:
                        pv(u - 1)
                    if 2 <= u < 9:
                        oT(u - 2)
                    if u in XA_BLOCKS:
                        b = XA_BLOCKS[u]
                        pe.wait_ge(xa_dve.sem, xa_dve.at(l, f"oT{2 * b + 1}"))
                        down(l, B_O + b, a_hi, a_lo, (2 * b, 2 * b + 1), b == 0, False,
                             between=(lambda: oT(7)) if b == 2 else None)
                pe.wait_ge(xa_dve.sem, xa_dve.at(l, "oT7"))
                last_down(l, B_O + 3, a_hi, a_lo, (6, 7), 2)

            pe.sem_inc(s_blk, SLOTS)
            pe.wait_ge(s_id, 16)
            pe.wait_ge(s_x[0], 16)
            x_transposes(range(4))
            with pe.Fori(0, L) as l:
                ffn(l, 0)
                mixer(l)
                cross(l)
                ffn(l, 1)


def kernel(**inputs):
    import numpy as np
    import concourse.bacc as bacc
    from concourse.bass_utils import run_bass_kernel_spmd

    a = {k: np.asarray(v) for k, v in inputs.items()}

    def chunks(w, cols):
        k = w.shape[0] // P
        return w.reshape(k, P, cols).transpose(1, 0, 2).reshape(P, k * cols)

    stream = np.zeros((L * NB + AHEAD, P, BLOCK), np.float32)
    at = 0

    def put(w):
        nonlocal at
        c = chunks(w, w.shape[1])
        stream[at, :, :c.shape[1]] = c
        at += 1

    def put_wide(w):
        put(w[:D // 2])
        put(w[D // 2:])

    for l in range(L):
        def ffn(n):
            gate, up, down = (a[f"ffn{n}_w_{k}"][l] for k in ("gate", "up", "down"))
            for c in range(STEPS + 1):
                s = slice(c * CF, (c + 1) * CF)
                both = np.concatenate([gate[:, s], up[:, s]], 1)
                if c == 0 and n == 1:
                    for k, end in PIECES:
                        put(both[k * P:end * P])
                    put(both[D // 2:])
                elif c < STEPS:
                    put_wide(both)
                if c:
                    put(down[(c - 1) * CF:c * CF])

        ffn(1)
        w = a["w_in"][l]
        for c in (3 * N, 4 * N):
            put_wide(w[:, c:c + N])
        put(w[:, 5 * N:5 * N + CC])
        for c in (0, N, 2 * N):
            put_wide(w[:, c:c + N])
        for c in range(0, 2 * D, N):
            put_wide(a["xa_wkv"][l][:, c:c + N])
        for k in OUT_ORDER:
            put(a["w_out"][l][k * 2 * P:(k + 1) * 2 * P])
        for c in (0, N):
            put_wide(a["xa_wq"][l][:, c:c + N])
        for k in range(4):
            put(a["xa_wo"][l][k * 2 * P:(k + 1) * 2 * P])
        ffn(2)
    assert at == L * NB

    par = np.empty((L, P, NPAR), np.float32)
    for l in range(L):
        for n, name in enumerate(NORMS):
            par[l, :, C_GAIN + 8 * n:C_GAIN + 8 * n + 8] = a[name][l].reshape(8, P).T
        par[l, :, C_SUB] = a["diff_subln"][l]
        for c in range(2):
            ch = slice(c * P, (c + 1) * P)
            par[l, :, C_CCW + c * KC:C_CCW + (c + 1) * KC] = a["cc_dw"][l][:, ch].T
            par[l, :, C_CCB + c] = a["cc_dw_b"][l][ch]
            par[l, :, C_LNG + c] = a["cc_ln_g"][l][ch]
            par[l, :, C_LNB + c] = a["cc_ln_b"][l][ch]
            par[l, :, C_SCW + c * KS:C_SCW + (c + 1) * KS] = a["sc_dw"][l][:, ch].T
        for n, name in enumerate(("lam_q1", "lam_k1", "lam_q2", "lam_k2")):
            par[l, :, C_LAM + n * DK:C_LAM + (n + 1) * DK] = a[name][l]
        par[l, :, C_INIT] = 0.8 - 0.6 * float(np.exp(-0.3 * l))
        par[l, :, C_REST] = 1.0 - (0.8 - 0.6 * float(np.exp(-0.3 * l)))

    const = np.zeros((P, NCONST), np.float32)
    const[:, K_ID:K_ID + P] = np.eye(P)
    const[:, K_MEAN:K_MEAN + P] = 1.0 / CC
    for t in range(TT):
        dist = (t * P + np.arange(P))[:, None] - np.arange(T)[None, :]
        const[:, K_DIST + t * T:K_DIST + (t + 1) * T] = np.where(dist >= 0, dist, MASKED)

    arrays = {
        "x_dram": np.ascontiguousarray(a["x"].reshape(T, D)),
        "mem_dram": np.ascontiguousarray(a["mem"].reshape(T, D)),
        "memT_dram": np.ascontiguousarray(a["mem"].reshape(T, KD, P).transpose(2, 1, 0)),
        "w_dram": stream,
        "par_dram": par,
        "const_dram": const,
        "fin_dram": np.ascontiguousarray(np.broadcast_to(a["final_norm"][None, :], (P, D))),
    }
    nc = bacc.Bacc("TRN2", target_bir_lowering=False, num_devices=1)
    args = [nc.dram_tensor(k, v.shape, F32, kind="ExternalInput").ap() for k, v in arrays.items()]
    out = nc.dram_tensor("out_dram", (T, D), F32, kind="ExternalOutput").ap()
    hymba_kernel(nc, *args, out)
    r = run_bass_kernel_spmd(nc, [arrays], core_ids=[0])
    return r.results[0]["out_dram"].reshape(1, T, D)
```
